# Optimizing a Trainium2 kernel written in Bass

```python
import jax, jax.numpy as jnp
from jax import lax
import numpy as np

D_MODEL = 1024
BATCH = 1
SEQ = 256
DEPTH = 2

A_HEADS = 8
A_HEAD_DIM = 64
A_LATENT = 128
IDX_HEADS = 8
IDX_DIM = 32
TOPK_MAX = 256
Q_BLOCK = 128
R_HEADS = 4
R_DK = 128
R_DV = 128
R_CHUNK = 128
CONV_WIDTH = 31
P_HEADS = 8
P_NKEYS = 128
P_EXPERTS = P_NKEYS * P_NKEYS
P_QDIM = 256
P_TOPK = 16
P_TOKEN_BLOCK = 128
EPS = 1e-6
IN_SIZES = (A_HEADS * A_HEAD_DIM,
            A_LATENT,
            IDX_HEADS * IDX_DIM,
            IDX_DIM,
            IDX_HEADS,
            R_HEADS * R_DK,
            R_HEADS * R_DK,
            R_HEADS * R_DV,
            R_HEADS * R_DV)
W_IN_COLS = sum(IN_SIZES)
MIX_WIDTH = A_HEADS * A_HEAD_DIM + R_HEADS * R_DV

kernel_name = 'hybrid_dsa_retention_conformer_peer'

def rms_norm(x, g):
    xf = x.astype(jnp.float32)
    y = xf * lax.rsqrt(jnp.mean(xf * xf, axis=-1, keepdims=True) + EPS)
    return (y * g.astype(jnp.float32)).astype(x.dtype)

def layer_norm(x, g, b):
    xf = x.astype(jnp.float32)
    mu = jnp.mean(xf, axis=-1, keepdims=True)
    var = jnp.mean(jnp.square(xf - mu), axis=-1, keepdims=True)
    y = (xf - mu) * lax.rsqrt(var + EPS)
    return (y * g.astype(jnp.float32) + b.astype(jnp.float32)).astype(x.dtype)

def dsa_sparse_attention(q_a, c_kv, q_idx, k_idx, w_idx, w_uk, w_uv):
    B, L, _ = q_a.shape
    topk = min(TOPK_MAX, L // 4)
    n_blk = L // Q_BLOCK
    q_a = q_a.reshape(B, L, A_HEADS, A_HEAD_DIM)
    q_lat = jnp.einsum('bshd,hcd->bshc', q_a, w_uk)
    q_idx = q_idx.reshape(B, L, IDX_HEADS, IDX_DIM)
    w_idx = w_idx * (IDX_HEADS ** -0.5)
    to_blocks = lambda t: t.reshape((B, n_blk, Q_BLOCK) + t.shape[2:]).swapaxes(0, 1)
    key_pos = jnp.arange(L)
    scale = A_HEAD_DIM ** -0.5

    def block(args):
        ql, qi, wi, blk = args
        q_pos = blk * Q_BLOCK + jnp.arange(Q_BLOCK)
        rel = jax.nn.relu(jnp.einsum('bqhd,bsd->bqhs', qi, k_idx))
        score = jnp.einsum('bqhs,bqh->bqs', rel, wi)
        causal = key_pos[None, :] <= q_pos[:, None]
        score = jnp.where(causal[None], score, -jnp.inf)
        _, idx = lax.top_k(score, topk)
        valid = idx <= q_pos[None, :, None]
        c_sel = jax.vmap(lambda c, i: c[i])(c_kv, idx)
        logits = jnp.einsum('bqhc,bqkc->bqhk', ql, c_sel).astype(jnp.float32) * scale
        logits = jnp.where(valid[:, :, None, :], logits, -jnp.inf)
        p = jax.nn.softmax(logits, axis=-1).astype(c_sel.dtype)
        return jnp.einsum('bqhk,bqkc->bqhc', p, c_sel)

    o_lat = lax.map(block, (to_blocks(q_lat), to_blocks(q_idx), to_blocks(w_idx),
                            jnp.arange(n_blk)))
    o_lat = o_lat.swapaxes(0, 1).reshape(B, L, A_HEADS, A_LATENT)
    out = jnp.einsum('bshc,hcd->bshd', o_lat, w_uv)
    return out.reshape(B, L, A_HEADS * A_HEAD_DIM)

def rotary(x):
    L, d = x.shape[1], x.shape[-1]
    inv_freq = 1.0 / (10000.0 ** jnp.linspace(0.0, 1.0, d // 2, dtype=jnp.float32))
    ang = jnp.arange(L, dtype=jnp.float32)[:, None] * inv_freq[None, :]
    cos = jnp.cos(ang)[None, :, None, :]
    sin = jnp.sin(ang)[None, :, None, :]
    x1 = x[..., 0::2]
    x2 = x[..., 1::2]
    return jnp.stack([x1 * cos - x2 * sin, x1 * sin + x2 * cos], axis=-1).reshape(x.shape)

def chunkwise_retention(q, k, v):
    B, L, _ = q.shape
    C = R_CHUNK
    N = L // C
    f32 = jnp.float32
    q = rotary(q.astype(f32).reshape(B, L, R_HEADS, R_DK))
    k = rotary(k.astype(f32).reshape(B, L, R_HEADS, R_DK)) * (R_DK ** -0.5)
    v = v.astype(f32).reshape(B, L, R_HEADS, R_DV)
    log_g = jnp.log1p(-jnp.exp2(-5.0 - jnp.arange(R_HEADS, dtype=f32)))
    pos = jnp.arange(C, dtype=f32)
    diff = pos[:, None] - pos[None, :]
    decay = jnp.where(diff >= 0, jnp.exp(jnp.maximum(diff, 0.0)[None] * log_g[:, None, None]), 0.0)
    xi = jnp.exp((pos + 1.0)[None, :] * log_g[:, None])
    zeta = jnp.exp((C - 1.0 - pos)[None, :] * log_g[:, None])
    g_chunk = jnp.exp(C * log_g)
    chunks = lambda t: t.reshape(B, N, C, R_HEADS, t.shape[-1]).transpose(1, 0, 3, 2, 4)
    qc, kc, vc = chunks(q), chunks(k), chunks(v)
    inner = jnp.einsum('nbhce,nbhse->nbhcs', qc, kc) * decay
    inner = jnp.einsum('nbhcs,nbhse->nbhce', inner, vc)

    def step(state, inp):
        qn, kn, vn = inp
        cross = jnp.einsum('bhcd,bhde->bhce', qn, state) * xi[None, :, :, None]
        state = state * g_chunk[None, :, None, None] + jnp.einsum(
            'bhcd,bhce->bhde', kn * zeta[None, :, :, None], vn)
        return state, cross

    state0 = jnp.zeros((B, R_HEADS, R_DK, R_DV), f32)
    _, cross = lax.scan(step, state0, (qc, kc, vc))
    out = (inner + cross).transpose(1, 0, 3, 2, 4).reshape(B, L, R_HEADS, R_DV)
    mu = jnp.mean(out, axis=-1, keepdims=True)
    var = jnp.mean(jnp.square(out - mu), axis=-1, keepdims=True)
    return (out - mu) * lax.rsqrt(var + EPS)

def attention_retention_mixer(h, w_in, kv_norm, w_uk, w_uv, w_o):
    B, L, _ = h.shape
    proj = h @ w_in
    points = np.cumsum(IN_SIZES)[:-1].tolist()
    qa, ckv, qi, ki, wi, rq, rk, rv, rg = jnp.split(proj, points, axis=-1)
    ckv = rms_norm(ckv, kv_norm)
    a_out = dsa_sparse_attention(qa, ckv, qi, ki, wi, w_uk, w_uv)
    ret = chunkwise_retention(rq, rk, rv).reshape(B, L, R_HEADS * R_DV).astype(h.dtype)
    b_out = jax.nn.silu(rg) * ret
    return jnp.concatenate([a_out, b_out], axis=-1) @ w_o

def conformer_conv_module(h, w_pw1, b_pw1, w_dw, b_dw, ln_g, ln_b, w_pw2, b_pw2):
    D = h.shape[-1]
    a = h @ w_pw1 + b_pw1
    a = a[..., :D] * jax.nn.sigmoid(a[..., D:])
    y = lax.conv_general_dilated(a, w_dw[:, None, :], window_strides=(1,),
                                 padding=((CONV_WIDTH - 1, 0),),
                                 dimension_numbers=('NWC', 'WIO', 'NWC'),
                                 feature_group_count=D) + b_dw
    y = jax.nn.silu(layer_norm(y, ln_g, ln_b))
    return y @ w_pw2 + b_pw2

def peer_ffn(h, w_q, sub_keys, u, v):
    B, L, D = h.shape
    T = B * L
    xf = h.reshape(T, D)
    q = (xf @ w_q).reshape(T, P_HEADS, 2, P_QDIM // 2)
    s1 = jnp.einsum('thd,kd->thk', q[:, :, 0], sub_keys[0])
    s2 = jnp.einsum('thd,kd->thk', q[:, :, 1], sub_keys[1])
    v1, i1 = lax.top_k(s1, P_TOPK)
    v2, i2 = lax.top_k(s2, P_TOPK)
    cand = (v1[..., :, None] + v2[..., None, :]).reshape(T, P_HEADS, P_TOPK * P_TOPK)
    sv, ci = lax.top_k(cand, P_TOPK)
    e1 = jnp.take_along_axis(i1, ci // P_TOPK, axis=-1)
    e2 = jnp.take_along_axis(i2, ci % P_TOPK, axis=-1)
    eidx = (e1 * P_NKEYS + e2).reshape(T, P_HEADS * P_TOPK)
    gate = jax.nn.softmax(sv.astype(jnp.float32), axis=-1).astype(h.dtype).reshape(T, P_HEADS * P_TOPK)
    n_blk = T // P_TOKEN_BLOCK

    def block(args):
        xb, ib, gb = args
        hb = jnp.einsum('td,tkd->tk', xb, u[ib])
        act = jax.nn.gelu(hb, approximate=False) * gb
        return jnp.einsum('tk,tkd->td', act, v[ib])

    out = lax.map(block, (xf.reshape(n_blk, P_TOKEN_BLOCK, D),
                          eidx.reshape(n_blk, P_TOKEN_BLOCK, -1),
                          gate.reshape(n_blk, P_TOKEN_BLOCK, -1)))
    return out.reshape(B, L, D)

def setup_inputs(seed: int = 0) -> dict:
    key = jax.random.key(seed)
    ks = iter(jax.random.split(key, 32))
    n_even = (DEPTH + 1) // 2
    n_odd = DEPTH // 2
    D = D_MODEL

    def nrm(shape, scale):
        return jax.random.normal(next(ks), shape, jnp.float32) * scale

    def gain(shape):
        return 1.0 + nrm(shape, 0.01)

    return {
        'x': nrm((BATCH, SEQ, D), 1.0),
        'mix_norm_e': gain((n_even, D)),
        'w_in': nrm((n_even, D, W_IN_COLS), D ** -0.5),
        'kv_norm': gain((n_even, A_LATENT)),
        'w_uk': nrm((n_even, A_HEADS, A_LATENT, A_HEAD_DIM), A_HEAD_DIM ** -0.5),
        'w_uv': nrm((n_even, A_HEADS, A_LATENT, A_HEAD_DIM), A_LATENT ** -0.5),
        'w_o': nrm((n_even, MIX_WIDTH, D), MIX_WIDTH ** -0.5),
        'mix_norm_o': gain((n_odd, D)),
        'conv_w1': nrm((n_odd, D, 2 * D), D ** -0.5),
        'conv_b1': nrm((n_odd, 2 * D), 0.01),
        'conv_dw': nrm((n_odd, CONV_WIDTH, D), CONV_WIDTH ** -0.5),
        'conv_dw_b': nrm((n_odd, D), 0.01),
        'conv_ln_g': gain((n_odd, D)),
        'conv_ln_b': nrm((n_odd, D), 0.01),
        'conv_w2': nrm((n_odd, D, D), D ** -0.5),
        'conv_b2': nrm((n_odd, D), 0.01),
        'ffn_norm': gain((DEPTH, D)),
        'peer_wq': nrm((DEPTH, D, P_HEADS * P_QDIM), D ** -0.5),
        'peer_keys': nrm((DEPTH, 2, P_NKEYS, P_QDIM // 2), (P_QDIM // 2) ** -0.5),
        'peer_u': nrm((DEPTH, P_EXPERTS, D), D ** -0.5),
        'peer_v': nrm((DEPTH, P_EXPERTS, D), D ** -0.5),
        'final_norm': gain((D,)),
    }

def reference(x, mix_norm_e, w_in, kv_norm, w_uk, w_uv, w_o, mix_norm_o, conv_w1, conv_b1,
              conv_dw, conv_dw_b, conv_ln_g, conv_ln_b, conv_w2, conv_b2, ffn_norm,
              peer_wq, peer_keys, peer_u, peer_v, final_norm):
    for layer in range(DEPTH):
        j = layer // 2
        if layer % 2 == 0:
            h = rms_norm(x, mix_norm_e[j])
            x = x + attention_retention_mixer(h, w_in[j], kv_norm[j], w_uk[j], w_uv[j], w_o[j])
        else:
            h = rms_norm(x, mix_norm_o[j])
            x = x + conformer_conv_module(h, conv_w1[j], conv_b1[j], conv_dw[j], conv_dw_b[j],
                                          conv_ln_g[j], conv_ln_b[j], conv_w2[j], conv_b2[j])
        h = rms_norm(x, ffn_norm[layer])
        x = x + peer_ffn(h, peer_wq[layer], peer_keys[layer], peer_u[layer], peer_v[layer])
    return rms_norm(x, final_norm)


_drawn_inputs = setup_inputs


def setup_inputs(seed=0):
    import zlib

    import numpy as np

    out = dict(_drawn_inputs(seed))
    spreads = {}
    factors = {'kv_norm': 8.0,
     'mix_norm_o': 8.0,
     'conv_b1': 8.0,
     'conv_dw_b': 5.412,
     'conv_ln_g': 8.0,
     'conv_ln_b': 8.0,
     'conv_b2': 7.175,
     'ffn_norm': 8.0,
     'peer_wq': 3.087,
     'peer_keys': 3.084,
     'peer_u': 3.387,
     'peer_v': 3.053,
     'final_norm': 5.512}
    for name, (base, spread) in spreads.items():
        noise = np.random.default_rng([zlib.crc32(name.encode()), seed]).standard_normal(out[name].shape)
        drawn = base * np.exp(spread * noise) if base else spread * noise
        out[name] = __import__('jax').numpy.asarray(drawn.astype(out[name].dtype))
    for name, factor in factors.items():
        out[name] = (out[name] * factor).astype(out[name].dtype)
    return out
```

```python
import concourse.bass as bass
from concourse import mybir
from contextlib import ExitStack

import numpy as np

P = 128
D = 1024
KD = D // P
TILES = 2
SEQ = TILES * P
LAYERS = 2
A_HEADS, A_DIM, LATENT = 8, 64, 128
I_HEADS, I_DIM = 8, 32
TOPK = SEQ // 4
R_HEADS, R_D = 4, 128
TAPS = 31
HIST = TAPS - 1
P_HEADS, P_TOP = 8, 16
PICKS = P_HEADS * P_TOP
EPS = 1e-6
C_QA = 0
C_CKV = C_QA + A_HEADS * A_DIM
C_QI = C_CKV + LATENT
C_KI = C_QI + I_HEADS * I_DIM
C_WI = C_KI + I_DIM
C_RQ = C_WI + I_HEADS
C_RK = C_RQ + R_HEADS * R_D
C_RV = C_RK + R_HEADS * R_D
C_RG = C_RV + R_HEADS * R_D
C_END = C_RG + R_HEADS * R_D
W_CUTS = [C_CKV, C_RQ, C_QA, C_RQ, C_RK, C_RV, C_RG, C_END]
W_PARTS = [(C_CKV, C_RQ), (C_QA, C_CKV), (C_RQ, C_RK), (C_RK, C_RV), (C_RV, C_RG), (C_RG, C_END)]

RING = 16
BATCH = 4
HALF = D // 2
WCOLS = 256
WBUF = 2

MASKED = -(2.0 ** 126)
TAKEN = -(2.0 ** 127)
OFF = -1e30
LOWEST = -3e38

NORMS = [(0, 0), (0, 1), (1, 0), (1, 1), (2, 0), (3, 0), (2, 1), (3, 1), (4, 0), (4, 1)]
FIN = 8
X_OF_NORM = [0, 0, 1, 2, 3, 4, 5, 6, 7, 8]
W_O = 0
W_PHASE = [4, 12, 32, 52]
W_CONV = [20, 40]
CP_DW, CP_BA, CP_BG, CP_DWB, CP_G, CP_B = 0, KD * TAPS, KD * TAPS + KD, KD * TAPS + 2 * KD, KD * TAPS + 3 * KD, KD * TAPS + 4 * KD
CP = CP_B + KD


def hybrid_decoder_trunk_kernel(nc, x, gains, w_in, kv_norm, uk_t, uv_w, w_o, rot, decay,
                                w1, chan, w2, b2, wq, keys_t, experts0, experts1, out):
    f32, u32 = mybir.dt.float32, mybir.dt.uint32
    ALU, ACT, AX = mybir.AluOpType, mybir.ActivationFunctionType, mybir.AxisListType
    ds = bass.ds

    w_in_v = w_in.rearrange("(k p) c -> p k c", p=P)
    w_o_v = w_o.rearrange("(k p) c -> p k c", p=P)
    w1_v = w1.rearrange("(k p) c -> p k c", p=P)
    w2_v = w2.rearrange("(k p) c -> p k c", p=P)
    wq_v = [wq[i, :, :].rearrange("(k p) c -> p k c", p=P) for i in range(LAYERS)]
    table = [experts0, experts1]

    ctx = ExitStack()
    with ctx:
        def sb(name, shape, dt=f32):
            return ctx.enter_context(nc.sbuf_tensor(name, shape, dt))

        def sem(name):
            return ctx.enter_context(nc.semaphore(name))

        ring = sb("ring", [P, RING, 2 * D])
        x_tok = sb("x_tok", [P, TILES, D])
        h_tok = sb("h_tok", [P, TILES, D])
        h_t = sb("h_t", [P, KD, P])
        gain = sb("gain", [P, 2, D])
        wbuf = sb("wbuf", [P, WBUF, KD, WCOLS])
        conv_buf = sb("conv_buf", [P, KD * (HIST + P) + KD * P])
        glu = conv_buf[:, 0:KD * (HIST + P)].rearrange("p (k c) -> p k c", k=KD)
        y_t = conv_buf[:, KD * (HIST + P):].rearrange("p (k c) -> p k c", k=KD)
        z_t = h_t
        chan_sb = sb("chan_sb", [P, CP])
        gate_sig = sb("gate_sig", [P, 2, P])
        rstd_y = sb("rstd_y", [P, P])
        b2_row = sb("b2_row", [1, D])
        ones_row = sb("ones_row", [1, P])
        mean_w = sb("mean_w", [P, P])
        zeros = sb("zeros", [P, P])
        ident = sb("ident", [P, P])
        iota16 = sb("iota16", [P, P_TOP])
        eps = sb("eps", [P, 1])
        keys_sb = sb("keys_sb", [P, LAYERS, 2, P])
        q_t = sb("q_t", [P, 2, 2 * P])
        top_v = sb("top_v", [P, 2, P_TOP])
        top_i = sb("top_i", [P, 2, P_TOP], u32)
        rest = sb("rest", [P, 2, P])
        cand = sb("cand", [P, P_TOP, P_TOP])
        cand2 = sb("cand2", [P, P_TOP, P_TOP])
        best_v = sb("best_v", [P, P_TOP])
        best_i = sb("best_i", [P, P_TOP], u32)
        best_ab = sb("best_ab", [P, 2, P_TOP], u32)
        onehot = sb("onehot", [P, 2, P_TOP, P_TOP])
        e12 = sb("e12", [P, 2, P_TOP])
        lead = sb("lead", [P, 2, P_TOP])
        expo = sb("expo", [P, 2, P_TOP])
        expo_sum = sb("expo_sum", [P, 2])
        gates = sb("gates", [P, TILES, PICKS])
        eidx = sb("eidx", [P, TILES, PICKS], u32)
        idx_now = sb("idx_now", [P, 2, RING], u32)
        hb = sb("hb", [P, RING])
        ge = sb("ge", [P, RING])
        act_v = sb("act_v", [P, RING])
        diag = sb("diag", [P, 2 * BATCH, P])
        ss = sb("ss", [P, len(NORMS)])
        root = sb("root", [P, len(NORMS)])
        rstd = sb("rstd", [P, len(NORMS)])

        ring_flat = ring[:, :, :].rearrange("p r c -> p (r c)")
        at = [0]

        def in_ring(*dims):
            n = int(np.prod(dims))
            v = ring_flat[:, at[0]:at[0] + n]
            at[0] += n
            names = "abcd"[:len(dims)]
            sizes = {names[i]: dims[i] for i in range(len(dims) - 1)}
            return v if len(dims) == 1 else v.rearrange(f"p ({' '.join(names)}) -> p {' '.join(names)}", **sizes)

        w_sb = in_ring(KD, C_END)
        at[0] = 0
        logit = in_ring(A_HEADS * SEQ)
        p_t = in_ring(2, A_HEADS * P)
        o_t = in_ring(A_HEADS * P)
        rel = in_ring(I_HEADS * SEQ)
        relw = in_ring(I_HEADS * SEQ)
        s_t = in_ring(R_HEADS, 3 * P)
        ql_t = in_ring(A_HEADS * SEQ)
        b_tok = in_ring(TILES, R_HEADS * R_D)
        assert at[0] <= KD * C_END
        at[0] = KD * C_END
        qa_t = in_ring(4, SEQ)
        qi_t = in_ring(2, SEQ)
        ki_t = in_ring(SEQ)
        rqk = in_ring(2, 2, 2, SEQ)
        rv = in_ring(TILES, R_HEADS * R_D)
        rg = in_ring(TILES, R_HEADS * R_D)
        ukt_sb = in_ring(4, LATENT)
        uvw_sb = in_ring(A_HEADS * A_DIM)
        c_tok = in_ring(TILES, LATENT)
        c_t = in_ring(SEQ)
        wi = in_ring(TILES, I_HEADS)
        rot_sb = in_ring(2, SEQ)
        score = in_ring(TILES, SEQ)
        assert at[0] <= RING * 2 * D, at[0]
        h_t2 = conv_buf[:, 0:KD * SEQ].rearrange("p (k c) -> p k c", k=KD)
        mix_t = conv_buf[:, 0:TILES * KD * P].rearrange("p (t k c) -> p t k c", t=TILES, k=KD)
        z_flat = diag[:, :, :].rearrange("p k c -> p (k c)")
        rot_tmp = onehot[:, :, :, :].rearrange("p a b c -> p (a b c)")
        rot_tm2 = z_flat[:, 0:2 * SEQ]
        kvg = z_flat[:, 2 * SEQ:2 * SEQ + LATENT]
        ckv_raw = z_flat[:, 3 * SEQ:3 * SEQ + TILES * LATENT].rearrange("p (t c) -> p t c", t=TILES)
        decay_sb = wbuf[:, :, :, :].rearrange("p a k c -> p (a k c)")[:, 0:R_HEADS * 3 * P] \
            .rearrange("p (h c) -> p h c", h=R_HEADS)
        small = h_t[:, :, :].rearrange("p k c -> p (k c)")
        mask = small[:, 0:TILES * SEQ].rearrange("p (t c) -> p t c", t=TILES)
        taken = small[:, TILES * SEQ:TILES * SEQ + SEQ]
        n0 = (TILES + 1) * SEQ
        best8 = small[:, n0:n0 + 8]
        row_max = small[:, n0 + 8:n0 + 16]
        row_sum = small[:, n0 + 16:n0 + 24]
        row_inv = small[:, n0 + 24:n0 + 32]
        gn_stat = small[:, n0 + 32:n0 + 32 + 48].rearrange("p (g s) -> p g s", s=6)
        gn_mv = small[:, n0 + 80:n0 + 96].rearrange("p (g s) -> p g s", s=2)
        gn_root = small[:, n0 + 96:n0 + 104]
        gn_rstd = small[:, n0 + 104:n0 + 112]
        c_ss = small[:, n0 + 112:n0 + 114]
        c_root = small[:, n0 + 114:n0 + 116]
        c_rstd = small[:, n0 + 116:n0 + 118]

        acc = ctx.enter_context(nc.psum_tensor("acc", [P, HALF], f32))
        ps_s = ctx.enter_context(nc.psum_tensor("ps_s", [P, 2, 512], f32))
        ps_q = ps_s[:, :, 2 * P:4 * P]
        pm = ctx.enter_context(nc.psum_tensor("pm", [P, 4 * 512], f32))

        x_loaded = [sem(f"x_loaded{t}") for t in range(TILES)]
        w_in_loaded = [sem(f"w_in_loaded{i}") for i in range(len(W_PARTS))]
        rot_loaded, uk_loaded, small_loaded, decay_loaded = sem("rot_loaded"), sem("uk_loaded"), sem("small_loaded"), sem("decay_loaded")
        const_ready = sem("const_ready")
        gain_loaded = [sem(f"gain_loaded{i}") for i in range(2)]
        norm_root, h_ready, h_t_ps, h_t_ready = sem("norm_root"), sem("h_ready"), sem("h_t_ps"), sem("h_t_ready")
        x_ready = sem("x_ready")
        proj_ps = sem("proj_ps")
        proj_read = [sem(f"proj_read{b}") for b in range(4)]
        ckv_root, c_ready, c_t_ps, c_t_ready = sem("ckv_root"), sem("c_ready"), sem("c_t_ps"), sem("c_t_ready")
        idx_ps, rel_ready, score_ready, causal_ready = sem("idx_ps"), sem("rel_ready"), sem("score_ready"), sem("causal_ready")
        taken_ready, mask_ready = sem("taken_ready"), sem("mask_ready")
        rot_ready = sem("rot_ready")
        rg_sig = sem("rg_sig")
        ret_s_ps, ret_s_ready, ret_ps = sem("ret_s_ps"), sem("ret_s_ready"), sem("ret_ps")
        gn_var, gn_rooted, b_ready, b_t_ps, b_t_ready = sem("gn_var"), sem("gn_rooted"), sem("b_ready"), sem("b_t_ps"), sem("b_t_ready")
        ql_ps, ql_ready = sem("ql_ps"), sem("ql_ready")
        logit_ps, logit_ready, expo_ready, prob_ready = sem("logit_ps"), sem("logit_ready"), sem("attn_exp"), sem("prob_ready")
        p_t_ps, p_t_ready, o_ps, o_ready, a_ps, a_ready = (sem(n) for n in ("p_t_ps", "p_t_ready", "o_ps", "o_ready", "a_ps", "a_ready"))
        wo_ps, wo_read = sem("wo_ps"), sem("wo_read")
        w_loaded = [sem(f"w_loaded{i}") for i in range(WBUF)]
        q_ps, q_t_ready, s_ps, s_read, topk_on = sem("q_ps"), sem("q_t_ready"), sem("s_ps"), sem("s_read"), sem("topk_on")
        lead_ready, gate_exp, picks_ready = sem("lead_ready"), sem("gate_exp"), sem("picks_ready")
        gathered = [sem(f"gathered{r}") for r in range(RING)]
        idx_copied, may_gather = sem("idx_copied"), sem("may_gather")
        dots_ready, act_ready, diag_ready, v_added, v_multiplied = (sem(n) for n in ("dots_ready", "act_ready", "diag_ready", "v_added", "v_multiplied"))
        acc_closed = sem("acc_closed")
        pw_ps, sig_ready, glu_ready = sem("pw_ps"), sem("sig_ready"), sem("glu_ready")
        y_ready, mu_ps, yc_ready, ysq_ready, var_ps, root_ready, u_ready, zsig_ready, z_ready = (
            sem(n) for n in ("y_ready", "mu_ps", "yc_ready", "ysq_ready", "var_ps", "root_ready", "u_ready", "zsig_ready", "z_ready"))
        w2_ps, w2_read = sem("w2_ps"), sem("w2_read")
        stored = sem("stored")

        block = ctx.enter_context(nc.Block())

        PROJ = ([("ckv", t, 0) for t in range(TILES)] + [("qi", i, 0) for i in range(2)] + [("ki", 0, 0)]
                + [("qa", i, 1) for i in range(4)] + [("rot", i, 2 + i // 2) for i in range(4)]
                + [("rv", t, 4) for t in range(TILES)] + [("rg", t, 5) for t in range(TILES)])

        def job_of(kind, i=0):
            return next(n for n, (k, j, _) in enumerate(PROJ) if (k, j) == (kind, i))

        @block.sync
        def _(sp):
            for t in range(TILES):
                sp.dma_start(x_tok[:, t, :], x[t * P:(t + 1) * P, :]).then_inc(x_loaded[t], 16)
            sp.dma_start(gain[:, 0, :], gains[0:1, :].broadcast_to([P, D])).then_inc(gain_loaded[0], 16)
            sp.dma_start(gain[:, 1, :], gains[0:1, :].broadcast_to([P, D])).then_inc(gain_loaded[1], 16)
            for i, (a, b) in enumerate(W_PARTS):
                sp.dma_start(w_sb[:, :, a:b], w_in_v[:, :, a:b]).then_inc(w_in_loaded[i], 16)
                if i == 0:
                    sp.dma_start(kvg, kv_norm.broadcast_to([P, LATENT])).then_inc(uk_loaded, 16)
                    sp.dma_start(ukt_sb, uk_t).then_inc(uk_loaded, 16)
                    sp.dma_start(uvw_sb, uv_w).then_inc(uk_loaded, 16)
                    sp.dma_start(rot_sb, rot).then_inc(rot_loaded, 16)
                    sp.dma_start(decay_sb, decay).then_inc(decay_loaded, 16)
            sp.dma_start(keys_sb[:, :, :, :], keys_t).then_inc(small_loaded, 16)
            sp.dma_start(chan_sb[:, :], chan).then_inc(small_loaded, 16)
            sp.dma_start(b2_row[:, :], b2).then_inc(small_loaded, 16)

            def load_gain(e):
                sp.wait_ge(h_ready, e - 1)
                sp.dma_start(gain[:, e % 2, :], gains[NORMS[e][0]:NORMS[e][0] + 1, :].broadcast_to([P, D])) \
                  .then_inc(gain_loaded[e % 2], 16)

            def multiplied(n):
                if n < W_PHASE[0]:
                    return wo_ps, TILES * (n + 1)
                for p, first in enumerate(W_PHASE):
                    if first <= n < first + P_HEADS:
                        return q_ps, p * P_HEADS + n - first + 1
                for t, first in enumerate(W_CONV):
                    if first <= n < first + KD:
                        return pw_ps, t * KD + n - first + 1
                    if first + KD <= n < first + KD + 4:
                        return w2_ps, t * 4 + n - first - KD + 1

            def load_chunks(view, first, count):
                for c in range(count):
                    n = first + c
                    if n >= WBUF:
                        sp.wait_ge(*multiplied(n - WBUF))
                    else:
                        sp.wait_ge(ret_s_ready, 1)
                    sp.dma_start(wbuf[:, n % WBUF, :, :], view[:, :, c * WCOLS:(c + 1) * WCOLS]) \
                      .then_inc(w_loaded[n % WBUF], 16)

            def load_conv(t):
                load_chunks(w1_v, W_CONV[t], KD)
                load_chunks(w2_v, W_CONV[t] + KD, 4)

            load_gain(2)
            load_gain(3)
            load_chunks(w_o_v, W_O, 4)
            load_chunks(wq_v[0], W_PHASE[0], P_HEADS)
            load_gain(4)
            load_chunks(wq_v[0], W_PHASE[1], P_HEADS)
            load_gain(5)
            load_conv(0)
            load_gain(6)
            load_chunks(wq_v[1], W_PHASE[2], P_HEADS)
            load_gain(7)
            load_conv(1)
            load_gain(8)
            load_chunks(wq_v[1], W_PHASE[3], P_HEADS)
            load_gain(9)
            for t in range(TILES):
                sp.wait_ge(h_ready, FIN + t + 1)
                sp.dma_start(out[t * P:(t + 1) * P, :], h_tok[:, t, :]).then_inc(stored, 16)
            sp.wait_ge(stored, 16 * TILES)

        @block.gpsimd
        def _(pool):
            pool.memset(ident[:, :], 1.0)
            pool.memset(zeros[:, :], 0.0)
            pool.memset(mean_w[:, :], 1.0 / D)
            pool.memset(ones_row[:, :], 1.0)
            pool.memset(eps[:, :], EPS)
            pool.iota(iota16[:, :], [[1, P_TOP]], base=0, channel_multiplier=0,
                      allow_small_or_imprecise_dtypes=True).then_inc(const_ready, 1)
            pool.wait_ge(const_ready, 1)
            pool.affine_select(out=ident[:, :], in_=ident[:, :], compare_op=ALU.is_equal, fill=0.0, base=0,
                               pattern=[[-1, P]], channel_multiplier=1).then_inc(const_ready, 1)
            for t in range(TILES):
                s = P * (t + 1)
                for src, ready, fill, done in ((score, score_ready, MASKED, causal_ready), (mask, taken_ready, OFF, mask_ready)):
                    pool.wait_ge(ready, t + 1)
                    pool.affine_select(out=src[:, t, 0:s], in_=src[:, t, 0:s], compare_op=ALU.is_ge, fill=fill,
                                       base=P * t, pattern=[[-1, s]], channel_multiplier=1).then_inc(done, 1)

            def gathers(p):
                layer, t = p // 2, p % 2
                rounds = PICKS // RING
                with pool.Fori(0, rounds // 2) as i:
                    for half in range(2):
                        r0 = p * rounds + half
                        pool.wait_ge(picks_ready, i * 2 + (r0 + 1))
                        pool.wait_ge(v_added, i * (2 * RING) + (r0 * RING + 1))
                        pool.sem_inc(may_gather, 1)
                        pool.tensor_copy(idx_now[:, half, :], eidx[:, t, ds(i * (2 * RING) + half * RING, RING)]) \
                            .then_inc(idx_copied, 1)
                        pool.wait_ge(idx_copied, i * 2 + (r0 + 1))
                        for r in range(RING):
                            freed = r0 * RING + r + 1
                            pool.wait_ge(v_added, i * (2 * RING) + freed)
                            pool.wait_ge(v_multiplied, i * (2 * RING) + freed)
                            pool.sem_inc(may_gather, 1)
                            pool.indirect_dma_start(ring[:, r, :], None, table[layer],
                                                    bass.IndirectOffsetOnAxis(idx_now[:, half, r:r + 1], 0)) \
                                .then_inc(gathered[r], 16)

            pool.wait_ge(x_ready, 2)
            for p in range(2 * LAYERS):
                gathers(p)

        @block.scalar
        def _(act):
            def norm(e):
                t = NORMS[e][1]
                if e < 2:
                    act.wait_ge(x_loaded[t], 16)
                else:
                    act.wait_ge(x_ready, X_OF_NORM[e])
                act.activation(h_tok[:, t, :], x_tok[:, t, :], ACT.Square, accum_out=ss[:, e:e + 1])
                act.drain()
                act.activation(root[:, e:e + 1], ss[:, e:e + 1], ACT.Sqrt, bias=eps[:, :], scale=1.0 / D).then_inc(norm_root, 1)

            def keep_h_t(e, dst, half):
                act.wait_ge(h_t_ps, e + 1)
                act.copy(dst, pm[:, half * 1024:half * 1024 + 1024].rearrange("p (k c) -> p k c", k=KD)).then_inc(h_t_ready, 1)

            act.wait_ge(const_ready, 2)
            norm(0)
            norm(1)
            keep_h_t(0, h_t2[:, :, 0:P], 0)
            keep_h_t(1, h_t2[:, :, P:SEQ], 1)

            def read(kind, i=0):
                n = job_of(kind, i)
                act.wait_ge(proj_ps, n + 1)
                return pm[:, (n % 4) * 512:(n % 4) * 512 + 512], proj_read[n % 4]

            for t in range(TILES):
                ps, done = read("ckv", t)
                act.copy(ckv_raw[:, t, :], ps[:, 0:LATENT])
                act.mul(wi[:, t, :].rearrange("p (a b) -> p a b", a=4),
                        ps[:, LATENT:LATENT + I_HEADS].rearrange("p (b a) -> p a b", a=4), I_HEADS ** -0.5).then_inc(done, 1)
                act.drain()
                act.activation(c_tok[:, t, :], ckv_raw[:, t, :], ACT.Square, accum_out=c_ss[:, t:t + 1])
                act.drain()
                act.activation(c_root[:, t:t + 1], c_ss[:, t:t + 1], ACT.Sqrt, bias=eps[:, :], scale=1.0 / LATENT).then_inc(ckv_root, 1)
            for kind, n, dst in (("qi", 2, qi_t), ("ki", 1, None), ("qa", 4, qa_t)):
                for i in range(n):
                    ps, done = read(kind, i)
                    act.copy(ki_t if dst is None else dst[:, i, :], ps[:, 0:SEQ]).then_inc(done, 1)
            for t in range(TILES):
                ps, done = read("rv", t)
                act.copy(rv[:, t, :], ps[:, :]).then_inc(done, 1)
            for t in range(TILES):
                n = job_of("rg", t)
                act.wait_ge(proj_ps, n + 1)
                act.activation(rg[:, t, :], pm[:, (n % 4) * 512:(n % 4) * 512 + 512], ACT.Sigmoid).then_inc(rg_sig, 1)
            act.wait_ge(c_t_ps, 2)
            act.copy(c_t, ps_s[:, 0, 0:SEQ]).then_inc(c_t_ready, 1)
            for t in range(TILES):
                s = P * (t + 1)
                act.wait_ge(idx_ps, t + 1)
                if t:
                    act.wait_ge(score_ready, t)
                act.activation(rel[:, 0:I_HEADS * s].rearrange("p (a c) -> p a c", a=4),
                               pm[:, :].rearrange("p (a c) -> p a c", a=4)[:, :, 0:2 * s], ACT.Relu).then_inc(rel_ready, 1)
            act.wait_ge(gn_var, 1)
            act.activation(gn_root, gn_mv[:, :, 1:2].rearrange("p g s -> p (g s)"), ACT.Sqrt, bias=eps[:, :]).then_inc(gn_rooted, 1)
            act.wait_ge(b_t_ps, 1)
            act.copy(mix_t[:, :, 4:8, :], pm[:, 0:1024].rearrange("p (t k c) -> p t k c", t=2, k=4)).then_inc(b_t_ready, 1)
            act.wait_ge(ql_ps, 1)
            act.copy(ql_t, pm[:, :]).then_inc(ql_ready, 1)
            for t in range(TILES):
                n = A_HEADS * P * (t + 1)
                act.wait_ge(logit_ready, t + 1)
                act.activation(logit[:, 0:n], logit[:, 0:n], ACT.Exp).then_inc(expo_ready, 1)
                act.wait_ge(p_t_ps, t + 1)
                act.copy(p_t[:, 0:t + 1, :], pm[:, 0:n].rearrange("p (s c) -> p s c", s=t + 1)).then_inc(p_t_ready, 1)
                act.wait_ge(o_ps, t + 1)
                act.copy(o_t, pm[:, 0:1024]).then_inc(o_ready, 1)
                act.wait_ge(a_ps, t + 1)
                act.copy(mix_t[:, t, 0:4, :], pm[:, 1024:1536].rearrange("p (k c) -> p k c", k=4)).then_inc(a_ready, 1)

            def norm_h_t(e):
                norm(e)
                keep_h_t(e, h_t[:, :, :], e % 2 if e < 4 else 0)

            def queries(p):
                with act.Fori(0, P_HEADS // 2) as i:
                    for b in range(2):
                        u = p * P_HEADS + b
                        act.wait_ge(q_ps, i * 2 + (u + 1))
                        act.copy(q_t[:, b, :], ps_q[:, b, :]).then_inc(q_t_ready, 1)
                    for b in range(2):
                        act.wait_ge(lead_ready, i * 2 + (p * P_HEADS + b + 1))
                        act.activation(expo[:, b, :], lead[:, b, :], ACT.Exp, accum_out=expo_sum[:, b:b + 1]).then_inc(gate_exp, 1)

            def experts_of(p):
                t = p % 2
                rounds = PICKS // RING
                with act.Fori(0, rounds) as i:
                    for b in range(RING // BATCH):
                        n0 = p * PICKS + b * BATCH
                        c = slice(b * BATCH, (b + 1) * BATCH)
                        act.wait_ge(dots_ready, i * RING + (n0 + BATCH))
                        act.activation(ge[:, c], hb[:, c], ACT.Gelu)
                        act.drain()
                        for j in range(BATCH):
                            r = b * BATCH + j
                            last = act.activation(act_v[:, r:r + 1], ge[:, r:r + 1], ACT.Copy,
                                                  scale=gates[:, t, ds(i * RING + r, 1)])
                        last.then_inc(act_ready, BATCH)
                        act.drain()
                        act.wait_ge(v_multiplied, i * RING + (RING + n0 - BATCH))
                        for j in range(BATCH):
                            r = b * BATCH + j
                            act.activation(diag[:, (b % 2) * BATCH + j, :], ident[:, :], ACT.Copy,
                                           scale=act_v[:, r:r + 1]).then_inc(diag_ready, 1)
                    act.drain()

            def conv(t):
                with act.Fori(0, KD // 2) as i:
                    for b in range(2):
                        n = t * KD + b
                        act.wait_ge(pw_ps, i * 2 + (n + 1))
                        act.wait_ge(glu_ready, i * 2 + (n + 1))
                        act.activation(gate_sig[:, b, :], pm[:, b * 1024 + P:b * 1024 + 2 * P], ACT.Sigmoid,
                                       bias=chan_sb[:, ds(i * 2 + (CP_BG + b), 1)]).then_inc(sig_ready, 1)
                act.wait_ge(yc_ready, t + 1)
                act.activation(z_t[:, :, :], y_t[:, :, :], ACT.Square).then_inc(ysq_ready, 1)
                act.wait_ge(var_ps, t + 1)
                act.activation(rstd_y[:, :], pm[:, P:2 * P], ACT.Sqrt, bias=eps[:, :]).then_inc(root_ready, 1)
                act.wait_ge(u_ready, t + 1)
                act.activation(z_t[:, :, :], y_t[:, :, :], ACT.Sigmoid).then_inc(zsig_ready, 1)

            norm_h_t(2)
            queries(0)
            norm_h_t(3)
            queries(1)
            experts_of(0)
            norm_h_t(4)
            conv(0)
            norm_h_t(5)
            queries(2)
            experts_of(1)
            norm_h_t(6)
            conv(1)
            norm_h_t(7)
            queries(3)
            experts_of(2)
            norm(8)
            experts_of(3)
            norm(9)

        @block.vector
        def _(dve):
            def norm(e):
                t = NORMS[e][1]
                dve.wait_ge(norm_root, e + 1)
                dve.reciprocal(rstd[:, e:e + 1], root[:, e:e + 1])
                dve.drain()
                dve.wait_ge(gain_loaded[e % 2], 16 * (e // 2 + 1))
                dve.scalar_tensor_tensor(out=h_tok[:, t, :], in0=x_tok[:, t, :], scalar=rstd[:, e:e + 1],
                                         in1=gain[:, e % 2, :], op0=ALU.mult, op1=ALU.mult).then_inc(h_ready, 1)

            dve.sem_inc(s_read, 2)
            dve.sem_inc(glu_ready, 2)
            dve.sem_inc(v_added, RING)
            norm(0)
            norm(1)
            dve.wait_ge(uk_loaded, 48)
            for t in range(TILES):
                dve.wait_ge(ckv_root, t + 1)
                dve.reciprocal(c_rstd[:, t:t + 1], c_root[:, t:t + 1])
                dve.drain()
                dve.scalar_tensor_tensor(out=c_tok[:, t, :], in0=ckv_raw[:, t, :], scalar=c_rstd[:, t:t + 1],
                                         in1=kvg, op0=ALU.mult, op1=ALU.mult).then_inc(c_ready, 1)
            dve.wait_ge(rot_loaded, 16)
            for i in range(4):
                n = job_of("rot", i)
                dve.wait_ge(proj_ps, n + 1)
                ps = pm[:, (n % 4) * 512:(n % 4) * 512 + 512].rearrange("p (a c) -> p a c", a=2)
                for a in range(2):
                    dve.tensor_tensor(rot_tmp[:, a * SEQ:(a + 1) * SEQ], ps[:, a, :], rot_sb[:, 0, :], ALU.mult)
                    last = dve.tensor_tensor(rot_tm2[:, a * SEQ:(a + 1) * SEQ], ps[:, 1 - a, :], rot_sb[:, 1, :], ALU.mult)
                last.then_inc(proj_read[n % 4], 1)
                dve.drain()
                dve.tensor_tensor(rqk[:, i // 2, i % 2, 0, :], rot_tmp[:, 0:SEQ], rot_tm2[:, 0:SEQ], ALU.subtract)
                dve.tensor_tensor(rqk[:, i // 2, i % 2, 1, :], rot_tmp[:, SEQ:2 * SEQ], rot_tm2[:, SEQ:2 * SEQ],
                                  ALU.add).then_inc(rot_ready, 1)
                dve.drain()
            for t in range(TILES):
                n = job_of("rg", t)
                dve.wait_ge(rg_sig, t + 1)
                dve.tensor_tensor(rg[:, t, :], pm[:, (n % 4) * 512:(n % 4) * 512 + 512], rg[:, t, :], ALU.mult) \
                    .then_inc(proj_read[n % 4], 1)
            for t in range(TILES):
                s = P * (t + 1)
                dve.wait_ge(rel_ready, t + 1)
                dve.tensor_tensor(relw[:, 0:I_HEADS * s].rearrange("p (h s) -> p h s", h=I_HEADS),
                                  rel[:, 0:I_HEADS * s].rearrange("p (h s) -> p h s", h=I_HEADS),
                                  wi[:, t, :].unsqueeze(2).broadcast_to([P, I_HEADS, s]), ALU.mult)
                dve.drain()
                dve.tensor_reduce(score[:, t, 0:s], relw[:, 0:I_HEADS * s].rearrange("p (h s) -> p s h", h=I_HEADS),
                                  AX.X, ALU.add).then_inc(score_ready, 1)
                dve.drain()
            for t in range(TILES):
                s = P * (t + 1)
                dve.wait_ge(causal_ready, t + 1)
                for _ in range(TOPK // 8):
                    dve.max(best8, score[:, t, 0:s])
                    dve.drain()
                    dve.match_replace(score[:, t, 0:s], best8, score[:, t, 0:s], TAKEN)
                    dve.drain()
                dve.tensor_scalar(mask[:, t, 0:s], score[:, t, 0:s], TAKEN, OFF, ALU.not_equal, ALU.mult).then_inc(taken_ready, 1)
            dve.wait_ge(ret_s_ps, 1)
            dve.wait_ge(decay_loaded, 16)
            dve.tensor_tensor(s_t, pm[:, :].rearrange("p (h c) -> p h c", h=R_HEADS)[:, :, 0:3 * P], decay_sb,
                              ALU.mult).then_inc(ret_s_ready, 1)
            dve.wait_ge(ret_ps, 1)
            for g in range(TILES * R_HEADS):
                dve.bn_stats(gn_stat[:, g, :], pm[:, g * R_D:(g + 1) * R_D])
            dve.drain()
            for g in range(TILES * R_HEADS):
                last = dve.bn_aggr(gn_mv[:, g, :], gn_stat[:, g, :])
            last.then_inc(gn_var, 1)
            dve.wait_ge(gn_rooted, 1)
            dve.reciprocal(gn_rstd, gn_root)
            dve.drain()
            for g in range(TILES * R_HEADS):
                t, h = g // R_HEADS, g % R_HEADS
                dve.tensor_scalar(b_tok[:, t, h * R_D:(h + 1) * R_D], pm[:, g * R_D:(g + 1) * R_D],
                                  gn_mv[:, g, 0:1], gn_rstd[:, g:g + 1], ALU.subtract, ALU.mult)
            dve.drain()
            dve.tensor_tensor(b_tok, b_tok, rg, ALU.mult).then_inc(b_ready, 1)
            for t in range(TILES):
                s = P * (t + 1)
                n = A_HEADS * s
                lg = logit[:, 0:n].rearrange("p (h s) -> p h s", h=A_HEADS)
                dve.wait_ge(logit_ps, t + 1)
                dve.wait_ge(mask_ready, t + 1)
                dve.scalar_tensor_tensor(out=lg, in0=pm[:, 0:n].rearrange("p (h s) -> p h s", h=A_HEADS),
                                         scalar=A_DIM ** -0.5, in1=mask[:, t, 0:s].unsqueeze(1).broadcast_to([P, A_HEADS, s]),
                                         op0=ALU.mult, op1=ALU.add)
                dve.drain()
                dve.tensor_reduce(row_max, lg, AX.X, ALU.max)
                dve.drain()
                dve.tensor_tensor(lg, lg, row_max.unsqueeze(2).broadcast_to([P, A_HEADS, s]), ALU.subtract).then_inc(logit_ready, 1)
                dve.wait_ge(expo_ready, t + 1)
                dve.tensor_reduce(row_sum, lg, AX.X, ALU.add)
                dve.drain()
                dve.reciprocal(row_inv, row_sum)
                dve.drain()
                dve.tensor_tensor(lg, lg, row_inv.unsqueeze(2).broadcast_to([P, A_HEADS, s]), ALU.mult).then_inc(prob_ready, 1)
                dve.drain()
            for c in range(4):
                for t in range(TILES):
                    n = 2 * c + t
                    dve.wait_ge(wo_ps, n + 1)
                    xs = x_tok[:, t, c * WCOLS:(c + 1) * WCOLS]
                    dve.tensor_tensor(xs, xs, pm[:, (n % 4) * 512:(n % 4) * 512 + WCOLS], ALU.add).then_inc(wo_read, 1)
                    if c == 3:
                        dve.drain().then_inc(x_ready, 1)

            def topk(p, i, b):
                t, u = p % 2, p * P_HEADS + b
                dve.wait_ge(s_ps, i * 2 + (u + 1))
                dve.sem_inc(topk_on, 1)
                side = [ps_s[:, b, j * P:(j + 1) * P] for j in range(2)]
                for j in range(2):
                    dve.max(top_v[:, j, 0:8], side[j])
                dve.drain()
                for j in range(2):
                    dve.max_index(top_i[:, j, 0:8], top_v[:, j, 0:8], side[j])
                    last = dve.match_replace(rest[:, j, :], top_v[:, j, 0:8], side[j], LOWEST)
                last.then_inc(s_read, 1)
                dve.drain()
                for j in range(2):
                    dve.max(top_v[:, j, 8:16], rest[:, j, :])
                dve.drain()
                for j in range(2):
                    dve.max_index(top_i[:, j, 8:16], top_v[:, j, 8:16], rest[:, j, :])
                dve.tensor_tensor(cand[:, :, :], top_v[:, 0, :].unsqueeze(2).broadcast_to([P, P_TOP, P_TOP]),
                                  top_v[:, 1, :].unsqueeze(1).broadcast_to([P, P_TOP, P_TOP]), ALU.add)
                dve.drain()
                flat, flat2 = (v[:, :, :].rearrange("p a b -> p (a b)") for v in (cand, cand2))
                dve.max(best_v[:, 0:8], flat)
                dve.drain()
                dve.max_index(best_i[:, 0:8], best_v[:, 0:8], flat)
                dve.match_replace(flat2, best_v[:, 0:8], flat, LOWEST)
                dve.drain()
                dve.max(best_v[:, 8:16], flat2)
                dve.drain()
                dve.max_index(best_i[:, 8:16], best_v[:, 8:16], flat2)
                dve.tensor_scalar(lead[:, b, :], best_v[:, :], best_v[:, 0:1], None, ALU.subtract).then_inc(lead_ready, 1)
                dve.drain()
                dve.tensor_scalar(best_ab[:, 0, :], best_i[:, :], 4, None, ALU.logical_shift_right)
                dve.tensor_scalar(best_ab[:, 1, :], best_i[:, :], P_TOP - 1, None, ALU.bitwise_and)
                dve.drain()
                dve.tensor_tensor(onehot[:, :, :, :], best_ab[:, :, :].unsqueeze(3).broadcast_to([P, 2, P_TOP, P_TOP]),
                                  iota16[:, :].unsqueeze(1).unsqueeze(1).broadcast_to([P, 2, P_TOP, P_TOP]), ALU.is_equal)
                dve.drain()
                dve.tensor_tensor(onehot[:, :, :, :], onehot[:, :, :, :],
                                  top_i[:, :, :].unsqueeze(2).broadcast_to([P, 2, P_TOP, P_TOP]), ALU.mult)
                dve.drain()
                dve.tensor_reduce(e12[:, :, :], onehot[:, :, :, :], AX.X, ALU.add)
                dve.drain()
                dve.scalar_tensor_tensor(out=eidx[:, t, ds(i * (2 * P_TOP) + b * P_TOP, P_TOP)], in0=e12[:, 0, :],
                                         scalar=float(P), in1=e12[:, 1, :], op0=ALU.mult, op1=ALU.add)
                dve.drain()

            def queries(p):
                with dve.Fori(0, P_HEADS // 2) as i:
                    for b in range(2):
                        topk(p, i, b)
                    for b in range(2):
                        dve.wait_ge(gate_exp, i * 2 + (p * P_HEADS + b + 1))
                        dve.reciprocal(expo_sum[:, b:b + 1], expo_sum[:, b:b + 1])
                        dve.drain()
                        dve.tensor_scalar(gates[:, p % 2, ds(i * (2 * P_TOP) + b * P_TOP, P_TOP)], expo[:, b, :],
                                          expo_sum[:, b:b + 1], None, ALU.mult).then_inc(picks_ready, 1)
                    dve.drain()

            def experts_of(p):
                t = p % 2
                rounds = PICKS // RING
                xs = x_tok[:, t, 0:HALF]

                def dots(i, b):
                    for j in range(BATCH):
                        r = b * BATCH + j
                        dve.wait_ge(gathered[r], i * 16 + 16 * (p * rounds + 1))
                        dve.scalar_tensor_tensor(out=ring[:, r, 0:D], in0=ring[:, r, 0:D], scalar=1.0, in1=h_tok[:, t, :],
                                                 op0=ALU.mult, op1=ALU.mult, accum_out=hb[:, r:r + 1]).then_inc(dots_ready, 1)

                def add_v(i, b):
                    n0 = p * PICKS + b * BATCH
                    dve.wait_ge(act_ready, i * RING + (n0 + BATCH))
                    for j in range(BATCH):
                        r = b * BATCH + j
                        dve.scalar_tensor_tensor(out=xs, in0=ring[:, r, D:D + HALF], scalar=act_v[:, r:r + 1], in1=xs,
                                                 op0=ALU.mult, op1=ALU.add).then_inc(v_added, 1)
                        dve.drain()

                with dve.Fori(0, rounds) as i:
                    dots(i, 0)
                    for b in range(1, RING // BATCH):
                        dots(i, b)
                        add_v(i, b - 1)
                    add_v(i, RING // BATCH - 1)
                dve.wait_ge(acc_closed, p + 1)
                dve.tensor_copy(x_tok[:, t, HALF:D], acc[:, :]).then_inc(x_ready, 1)

            def conv(t):
                if t:
                    dve.tensor_copy(glu[:, :, 0:HIST], glu[:, :, P:P + HIST])
                    dve.drain()
                else:
                    dve.memset(glu[:, :, 0:HIST], 0.0)
                with dve.Fori(0, 2) as i:
                    for c in range(4):
                        n = t * KD + c
                        dve.wait_ge(sig_ready, i * 4 + (n + 1))
                        dve.scalar_tensor_tensor(out=glu[:, ds(i * 4 + c, 1), HIST:HIST + P].rearrange("p a c -> p (a c)"),
                                                 in0=pm[:, (c % 2) * 1024:(c % 2) * 1024 + P],
                                                 scalar=chan_sb[:, ds(i * 4 + (CP_BA + c), 1)],
                                                 in1=gate_sig[:, c % 2, :], op0=ALU.add, op1=ALU.mult).then_inc(glu_ready, 1)
                    dve.drain()
                    for w in range(TAPS):
                        for c in range(4):
                            src = glu[:, ds(i * 4 + c, 1), w:w + P].rearrange("p a c -> p (a c)")
                            dst = y_t[:, ds(i * 4 + c, 1), :].rearrange("p a c -> p (a c)")
                            tap = chan_sb[:, ds(i * (4 * TAPS) + (CP_DW + c * TAPS + w), 1)]
                            if w == 0:
                                dve.tensor_scalar(dst, src, tap, chan_sb[:, ds(i * 4 + (CP_DWB + c), 1)], ALU.mult, ALU.add)
                            else:
                                dve.scalar_tensor_tensor(out=dst, in0=src, scalar=tap, in1=dst, op0=ALU.mult, op1=ALU.add)
                        dve.drain()
                dve.drain().then_inc(y_ready, 1)
                dve.wait_ge(mu_ps, t + 1)
                dve.tensor_tensor(y_t[:, :, :], y_t[:, :, :], pm[:, 0:P].unsqueeze(1).broadcast_to([P, KD, P]),
                                  ALU.subtract).then_inc(yc_ready, 1)
                dve.wait_ge(root_ready, t + 1)
                dve.reciprocal(rstd_y[:, :], rstd_y[:, :])
                dve.drain()
                dve.tensor_tensor(y_t[:, :, :], y_t[:, :, :], rstd_y[:, :].unsqueeze(1).broadcast_to([P, KD, P]), ALU.mult)
                dve.drain()
                for c in range(KD):
                    last = dve.tensor_scalar(y_t[:, c, :], y_t[:, c, :], chan_sb[:, CP_G + c:CP_G + c + 1],
                                             chan_sb[:, CP_B + c:CP_B + c + 1], ALU.mult, ALU.add)
                last.then_inc(u_ready, 1)
                dve.wait_ge(zsig_ready, t + 1)
                dve.tensor_tensor(z_t[:, :, :], z_t[:, :, :], y_t[:, :, :], ALU.mult).then_inc(z_ready, 1)
                for c in range(4):
                    n = 4 * t + c
                    dve.wait_ge(w2_ps, n + 1)
                    xs = x_tok[:, t, c * WCOLS:(c + 1) * WCOLS]
                    dve.tensor_tensor(xs, xs, pm[:, (c % 2) * 1024:(c % 2) * 1024 + WCOLS], ALU.add).then_inc(w2_read, 1)
                dve.drain().then_inc(x_ready, 1)

            norm(2)
            dve.wait_ge(const_ready, 2)
            queries(0)
            norm(3)
            queries(1)
            experts_of(0)
            norm(4)
            dve.wait_ge(small_loaded, 48)
            conv(0)
            norm(5)
            queries(2)
            experts_of(1)
            norm(6)
            conv(1)
            norm(7)
            queries(3)
            experts_of(2)
            norm(8)
            experts_of(3)
            norm(9)

        @block.tensor
        def _(pe):
            def transpose_h(e, half):
                t = NORMS[e][1]
                pe.wait_ge(h_ready, e + 1)
                for k in range(KD):
                    last = pe.transpose(pm[:, half * 1024 + k * P:half * 1024 + (k + 1) * P], h_tok[:, t, k * P:(k + 1) * P], ident[:, :])
                last.then_inc(h_t_ps, 1)

            def product(dst, lhs, rhs):
                for k in range(KD):
                    last = pe.matmul(dst, lhs(k), rhs(k), start=(k == 0), stop=(k == KD - 1))
                return last

            pe.sem_inc(v_multiplied, RING)
            pe.wait_ge(const_ready, 2)
            transpose_h(0, 0)
            transpose_h(1, 1)
            pe.wait_ge(h_t_ready, 2)
            for n, (kind, i, part) in enumerate(PROJ):
                pe.wait_ge(w_in_loaded[part], 16)
                if n >= 4:
                    pe.wait_ge(proj_read[n % 4], n // 4)
                ps = pm[:, (n % 4) * 512:(n % 4) * 512 + 512]
                if kind == "ckv":
                    tok = slice(i * P, (i + 1) * P)
                    product(ps[:, 0:LATENT], lambda k: h_t2[:, k, tok], lambda k: w_sb[:, k, C_CKV:C_CKV + LATENT])
                    last = product(ps[:, LATENT:LATENT + I_HEADS], lambda k: h_t2[:, k, tok], lambda k: w_sb[:, k, C_WI:C_WI + I_HEADS])
                elif kind == "qi":
                    last = product(ps[:, 0:SEQ], lambda k: w_sb[:, k, C_QI + i * P:C_QI + (i + 1) * P], lambda k: h_t2[:, k, :])
                elif kind == "ki":
                    for g in range(4):
                        last = product(ps[g * I_DIM:(g + 1) * I_DIM, 0:SEQ], lambda k: w_sb[:, k, C_KI:C_KI + I_DIM], lambda k: h_t2[:, k, :])
                elif kind == "qa":
                    last = product(ps[:, 0:SEQ], lambda k: w_sb[:, k, C_QA + i * P:C_QA + (i + 1) * P], lambda k: h_t2[:, k, :])
                elif kind == "rot":
                    c0 = (C_RQ, C_RK)[i // 2] + (i % 2) * 2 * R_D
                    for a in range(2):
                        last = product(ps[:, a * SEQ:(a + 1) * SEQ], lambda k: w_sb[:, k, c0 + a:c0 + a + 2 * R_D - 1:2], lambda k: h_t2[:, k, :])
                else:
                    tok = slice(i * P, (i + 1) * P)
                    c0 = C_RV if kind == "rv" else C_RG
                    last = product(ps[:, :], lambda k: h_t2[:, k, tok], lambda k: w_sb[:, k, c0:c0 + R_HEADS * R_D])
                last.then_inc(proj_ps, 1)
            for t in range(TILES):
                pe.wait_ge(c_ready, t + 1)
                pe.transpose(ps_s[:, 0, t * P:(t + 1) * P], c_tok[:, t, :], ident[:, :]).then_inc(c_t_ps, 1)
            for b in range(4):
                pe.wait_ge(proj_read[b], sum(1 for n in range(len(PROJ)) if n % 4 == b))
            for t in range(TILES):
                s = P * (t + 1)
                if t:
                    pe.wait_ge(rel_ready, t)
                for h in range(I_HEADS):
                    rows = slice((h % 4) * I_DIM, (h % 4 + 1) * I_DIM)
                    c0 = (h % 4) * 512 + (h // 4) * s
                    last = pe.matmul(pm[:, c0:c0 + s], qi_t[rows, h // 4, t * P:(t + 1) * P], ki_t[rows, 0:s], start=True, stop=True)
                last.then_inc(idx_ps, 1)
            pe.wait_ge(rel_ready, 2)
            pe.wait_ge(rot_ready, 4)
            for h in range(R_HEADS):
                rows = slice((h % 2) * 64, (h % 2) * 64 + 64)
                for n, (s, c) in enumerate(((0, 0), (1, 1), (0, 1))):
                    for a in range(2):
                        last = pe.matmul(pm[:, h * 512 + n * P:h * 512 + (n + 1) * P],
                                         rqk[rows, 1, h // 2, a, s * P:(s + 1) * P], rqk[rows, 0, h // 2, a, c * P:(c + 1) * P],
                                         start=(a == 0), stop=(a == 1))
            last.then_inc(ret_s_ps, 1)
            pe.wait_ge(ret_s_ready, 1)
            for t in range(TILES):
                for h in range(R_HEADS):
                    dst = pm[:, t * 512 + h * R_D:t * 512 + (h + 1) * R_D]
                    v = slice(h * R_D, (h + 1) * R_D)
                    if t == 0:
                        last = pe.matmul(dst, s_t[:, h, 0:P], rv[:, 0, v], start=True, stop=True)
                    else:
                        pe.matmul(dst, s_t[:, h, 2 * P:3 * P], rv[:, 0, v], start=True, stop=False)
                        last = pe.matmul(dst, s_t[:, h, P:2 * P], rv[:, 1, v], start=False, stop=True)
            last.then_inc(ret_ps, 1)
            pe.wait_ge(b_ready, 1)
            for t in range(TILES):
                for h in range(R_HEADS):
                    last = pe.transpose(pm[:, t * 512 + h * P:t * 512 + (h + 1) * P], b_tok[:, t, h * R_D:(h + 1) * R_D], ident[:, :])
            last.then_inc(b_t_ps, 1)
            pe.wait_ge(b_t_ready, 1)
            pe.wait_ge(uk_loaded, 48)

            def ql_at(h):
                return (h % 2) * 1024 + (h // 2) * SEQ

            for h in range(A_HEADS):
                rows = slice((h % 2) * A_DIM, (h % 2 + 1) * A_DIM)
                last = pe.matmul(pm[:, ql_at(h):ql_at(h) + SEQ], ukt_sb[rows, h // 2, :], qa_t[rows, h // 2, :], start=True, stop=True)
            last.then_inc(ql_ps, 1)
            pe.wait_ge(ql_ready, 1)
            pe.wait_ge(c_t_ready, 1)
            for t in range(TILES):
                s = P * (t + 1)
                if t:
                    pe.wait_ge(a_ready, t)
                for h in range(A_HEADS):
                    last = pe.matmul(pm[:, h * s:(h + 1) * s], ql_t[:, ql_at(h) + t * P:ql_at(h) + (t + 1) * P], c_t[:, 0:s], start=True, stop=True)
                last.then_inc(logit_ps, 1)
                pe.wait_ge(prob_ready, t + 1)
                for k in range(t + 1):
                    for h in range(A_HEADS):
                        last = pe.transpose(pm[:, (k * A_HEADS + h) * P:(k * A_HEADS + h + 1) * P],
                                            logit[:, h * s + k * P:h * s + (k + 1) * P], ident[:, :])
                last.then_inc(p_t_ps, 1)
                pe.wait_ge(p_t_ready, t + 1)
                for half in range(2):
                    for k in range(t + 1):
                        last = pe.matmul(pm[:, half * 512:(half + 1) * 512], c_tok[:, k, :], p_t[:, k, half * 512:(half + 1) * 512],
                                         start=(k == 0), stop=(k == t))
                last.then_inc(o_ps, 1)
                pe.wait_ge(o_ready, t + 1)
                for h in range(A_HEADS):
                    last = pe.matmul(pm[(h % 2) * A_DIM:(h % 2 + 1) * A_DIM, 1024 + (h // 2) * P:1024 + (h // 2 + 1) * P],
                                     uvw_sb[:, h * A_DIM:(h + 1) * A_DIM], o_t[:, h * P:(h + 1) * P], start=True, stop=True)
                last.then_inc(a_ps, 1)

            def chunk(n):
                pe.wait_ge(w_loaded[n % WBUF], 16 * (n // WBUF + 1))
                return wbuf[:, n % WBUF, :, :]

            pe.wait_ge(a_ready, 2)
            for c in range(4):
                w = chunk(W_O + c)
                for t in range(TILES):
                    n = 2 * c + t
                    if n >= 4:
                        pe.wait_ge(wo_read, n - 3)
                    last = product(pm[:, (n % 4) * 512:(n % 4) * 512 + WCOLS], lambda k: mix_t[:, t, k, :], lambda k: w[:, k, :])
                    last.then_inc(wo_ps, 1)

            def norm_h_t(e):
                transpose_h(e, e % 2 if e < 4 else 0)

            def queries(p):
                e = (2, 3, 5, 7)[p]
                pe.wait_ge(h_t_ready, e + 1)
                if p == 0:
                    pe.wait_ge(small_loaded, 48)
                with pe.Fori(0, P_HEADS // 2) as i:
                    for b in range(2):
                        n, u = W_PHASE[p] + b, p * P_HEADS + b
                        pe.wait_ge(w_loaded[b], i * 16 + 16 * (n // 2 + 1))
                        pe.wait_ge(s_read, i * 2 + (u + 1))
                        for j in range(2):
                            last = product(ps_q[:, b, j * P:(j + 1) * P], lambda k: wbuf[:, b, k, j * P:(j + 1) * P], lambda k: h_t[:, k, :])
                        last.then_inc(q_ps, 1)
                    for b in range(2):
                        u = p * P_HEADS + b
                        pe.wait_ge(q_t_ready, i * 2 + (u + 1))
                        for j in range(2):
                            last = pe.matmul(ps_s[:, b, j * P:(j + 1) * P], q_t[:, b, j * P:(j + 1) * P], keys_sb[:, p // 2, j, :], start=True, stop=True)
                        last.then_inc(s_ps, 1)

            def experts_of(p):
                t = p % 2
                xs = x_tok[:, t, HALF:D]
                if p:
                    pe.wait_ge(x_ready, {1: 3, 2: 5, 3: 7}[p])
                pe.matmul(acc[:, :], ident[:, :], xs, start=True, stop=False)
                with pe.Fori(0, PICKS // RING) as i:
                    for r in range(RING):
                        n = p * PICKS + r
                        pe.wait_ge(diag_ready, i * RING + (n + 1))
                        pe.matmul(acc[:, :], diag[:, r % (2 * BATCH), :], ring[:, r, D + HALF:2 * D], start=False, stop=False) \
                            .then_inc(v_multiplied, 1)
                pe.matmul(acc[:, :], zeros[:, :], xs, start=False, stop=True).then_inc(acc_closed, 1)

            def conv(t):
                e = (4, 6)[t]
                pe.wait_ge(h_t_ready, e + 1)
                with pe.Fori(0, KD // 2) as i:
                    for b in range(2):
                        n, m = W_CONV[t] + b, t * KD + b
                        pe.wait_ge(w_loaded[b], i * 16 + 16 * (n // 2 + 1))
                        pe.wait_ge(glu_ready, i * 2 + (m + 1))
                        for j in range(2):
                            last = product(pm[:, b * 1024 + j * P:b * 1024 + (j + 1) * P], lambda k: wbuf[:, b, k, j * P:(j + 1) * P], lambda k: h_t[:, k, :])
                        last.then_inc(pw_ps, 1)
                pe.wait_ge(y_ready, t + 1)
                product(pm[:, 0:P], lambda k: mean_w[:, :], lambda k: y_t[:, k, :]).then_inc(mu_ps, 1)
                pe.wait_ge(ysq_ready, t + 1)
                product(pm[:, P:2 * P], lambda k: mean_w[:, :], lambda k: z_t[:, k, :]).then_inc(var_ps, 1)
                pe.wait_ge(z_ready, t + 1)
                for c in range(4):
                    n = 4 * t + c
                    w = chunk(W_CONV[t] + KD + c)
                    if c >= 2:
                        pe.wait_ge(w2_read, n - 1)
                    dst = pm[:, (c % 2) * 1024:(c % 2) * 1024 + WCOLS]
                    pe.matmul(dst, ones_row[:, :], b2_row[:, c * WCOLS:(c + 1) * WCOLS], start=True, stop=False)
                    for k in range(KD):
                        last = pe.matmul(dst, z_t[:, k, :], w[:, k, :], start=False, stop=(k == KD - 1))
                    last.then_inc(w2_ps, 1)

            norm_h_t(2)
            queries(0)
            norm_h_t(3)
            queries(1)
            experts_of(0)
            norm_h_t(4)
            conv(0)
            norm_h_t(5)
            queries(2)
            experts_of(1)
            norm_h_t(6)
            conv(1)
            norm_h_t(7)
            queries(3)
            experts_of(2)
            experts_of(3)


def rotary_table():
    freq = (1.0 / (np.float32(10000.0) ** np.linspace(0.0, 1.0, R_D // 2, dtype=np.float32))).astype(np.float32)
    ang = (np.tile(freq, 2)[:, None] * np.arange(SEQ, dtype=np.float32)[None, :]).astype(np.float32)
    return np.stack([np.cos(ang), np.sin(ang)], axis=1).astype(np.float32)


def decay_table():
    log_g = np.log1p(-np.exp2(-5.0 - np.arange(R_HEADS)))
    diff = np.arange(P)[None, :] - np.arange(P)[:, None]
    near = np.where(diff[:, None, :] >= 0, np.exp(np.maximum(diff, 0)[:, None, :] * log_g[None, :, None]), 0.0)
    far = np.exp((diff + P)[:, None, :] * log_g[None, :, None])
    return (np.concatenate([near, near, far], axis=2) * R_D ** -0.5).astype(np.float32)


def kernel(**inputs):
    import concourse.bacc as bacc
    from concourse.bass_utils import run_bass_kernel_spmd

    a = {k: np.asarray(v) for k, v in inputs.items()}

    def channels(v):
        return v.reshape(-1, P).T

    taps = a["conv_dw"][0].T.reshape(KD, P, TAPS).transpose(1, 0, 2).reshape(P, KD * TAPS)
    arrays = {
        "x": a["x"][0],
        "gains": np.concatenate([a["mix_norm_e"], a["ffn_norm"][0:1], a["mix_norm_o"], a["ffn_norm"][1:2], a["final_norm"][None]]),
        "w_in": a["w_in"][0],
        "kv_norm": a["kv_norm"],
        "uk_t": a["w_uk"][0].transpose(0, 2, 1).reshape(4, P, LATENT).transpose(1, 0, 2),
        "uv_w": a["w_uv"][0].transpose(1, 0, 2).reshape(LATENT, A_HEADS * A_DIM),
        "w_o": a["w_o"][0],
        "rot": rotary_table(),
        "decay": decay_table(),
        "w1": a["conv_w1"][0].reshape(D, 2, KD, P).transpose(0, 2, 1, 3).reshape(D, 2 * D),
        "chan": np.concatenate([taps, channels(a["conv_b1"][0]), channels(a["conv_dw_b"][0]),
                                channels(a["conv_ln_g"][0]), channels(a["conv_ln_b"][0])], axis=1),
        "w2": a["conv_w2"][0],
        "b2": a["conv_b2"],
        "wq": a["peer_wq"],
        "keys_t": a["peer_keys"].transpose(3, 0, 1, 2),
        "experts0": np.concatenate([a["peer_u"][0], a["peer_v"][0]], axis=1),
        "experts1": np.concatenate([a["peer_u"][1], a["peer_v"][1]], axis=1),
    }
    arrays = {f"{n}_dram": np.ascontiguousarray(v) for n, v in arrays.items()}
    nc = bacc.Bacc("TRN2", target_bir_lowering=False, num_devices=1)
    args = [nc.dram_tensor(n, v.shape, mybir.dt.from_np(v.dtype), kind="ExternalInput").ap() for n, v in arrays.items()]
    out = nc.dram_tensor("out_dram", (SEQ, D), mybir.dt.float32, kind="ExternalOutput").ap()
    hybrid_decoder_trunk_kernel(nc, *args, out)
    r = run_bass_kernel_spmd(nc, [arrays], core_ids=[0])
    return r.results[0]["out_dram"].reshape(1, SEQ, D)
```

```python
import concourse.bass as bass
from concourse import mybir
from contextlib import ExitStack

import numpy as np

P = 128
D = 1024
KD = D // P
TILES = 2
SEQ = TILES * P
LAYERS = 2
A_HEADS, A_DIM, LATENT = 8, 64, 128
I_HEADS, I_DIM = 8, 32
TOPK = SEQ // 4
R_HEADS, R_D = 4, 128
TAPS = 31
HIST = TAPS - 1
P_HEADS, P_TOP = 8, 16
PICKS = P_HEADS * P_TOP
EPS = 1e-6
C_QA = 0
C_CKV = C_QA + A_HEADS * A_DIM
C_QI = C_CKV + LATENT
C_KI = C_QI + I_HEADS * I_DIM
C_WI = C_KI + I_DIM
C_RQ = C_WI + I_HEADS
C_RK = C_RQ + R_HEADS * R_D
C_RV = C_RK + R_HEADS * R_D
C_RG = C_RV + R_HEADS * R_D
C_END = C_RG + R_HEADS * R_D
W_CUTS = [C_CKV, C_RQ, C_QA, C_RQ, C_RK, C_RV, C_RG, C_END]
W_PARTS = [(C_CKV, C_RQ), (C_QA, C_CKV), (C_RQ, C_RK), (C_RK, C_RV), (C_RV, C_RG), (C_RG, C_END)]

RING = 16
BATCH = 4
HALF = D // 2
WCOLS = 256
WBUF = 2

MASKED = -(2.0 ** 126)
TAKEN = -(2.0 ** 127)
OFF = -1e30
LOWEST = -3e38

NORMS = [(0, 0), (0, 1), (1, 0), (1, 1), (2, 0), (3, 0), (2, 1), (3, 1), (4, 0), (4, 1)]
FIN = 8
X_OF_NORM = [0, 0, 1, 2, 3, 4, 5, 6, 7, 8]
W_O = 0
W_PHASE = [4, 12, 32, 52]
W_CONV = [20, 40]
CP_DW, CP_BA, CP_BG, CP_DWB, CP_G, CP_B = 0, KD * TAPS, KD * TAPS + KD, KD * TAPS + 2 * KD, KD * TAPS + 3 * KD, KD * TAPS + 4 * KD
CP = CP_B + KD


def hybrid_decoder_trunk_kernel(nc, x, gains, w_in, kv_norm, uk_t, uv_w, w_o, rot, decay,
                                w1, chan, w2, b2, wq, keys_t, experts0, experts1, out):
    f32, u32 = mybir.dt.float32, mybir.dt.uint32
    ALU, ACT, AX = mybir.AluOpType, mybir.ActivationFunctionType, mybir.AxisListType
    ds = bass.ds

    w_in_v = w_in.rearrange("(k p) c -> p k c", p=P)
    w_o_v = w_o.rearrange("(k p) c -> p k c", p=P)
    w1_v = w1.rearrange("(k p) c -> p k c", p=P)
    w2_v = w2.rearrange("(k p) c -> p k c", p=P)
    wq_v = [wq[i, :, :].rearrange("(k p) c -> p k c", p=P) for i in range(LAYERS)]
    table = [experts0, experts1]

    ctx = ExitStack()
    with ctx:
        def sb(name, shape, dt=f32):
            return ctx.enter_context(nc.sbuf_tensor(name, shape, dt))

        def sem(name):
            return ctx.enter_context(nc.semaphore(name))

        ring = sb("ring", [P, RING, 2 * D])
        x_tok = sb("x_tok", [P, TILES, D])
        h_tok = sb("h_tok", [P, TILES, D])
        h_t = sb("h_t", [P, KD, P])
        gain = sb("gain", [P, 2, D])
        wbuf = sb("wbuf", [P, WBUF, KD, WCOLS])
        conv_buf = sb("conv_buf", [P, KD * (HIST + P) + KD * P])
        glu = conv_buf[:, 0:KD * (HIST + P)].rearrange("p (k c) -> p k c", k=KD)
        y_t = conv_buf[:, KD * (HIST + P):].rearrange("p (k c) -> p k c", k=KD)
        z_t = h_t
        chan_sb = sb("chan_sb", [P, CP])
        gate_sig = sb("gate_sig", [P, 4, P])
        rstd_y = sb("rstd_y", [P, P])
        b2_row = sb("b2_row", [1, D])
        ones_row = sb("ones_row", [1, P])
        mean_w = sb("mean_w", [P, P])
        zeros = sb("zeros", [P, P])
        ident = sb("ident", [P, P])
        iota16 = sb("iota16", [P, P_TOP])
        eps = sb("eps", [P, 1])
        keys_sb = sb("keys_sb", [P, LAYERS, 2, P])
        q_t = sb("q_t", [P, 2, 2 * P])
        top_v = sb("top_v", [P, 2, P_TOP])
        top_i = sb("top_i", [P, 2, P_TOP], u32)
        rest = sb("rest", [P, 2, P])
        cand = sb("cand", [P, P_TOP, P_TOP])
        cand2 = sb("cand2", [P, P_TOP, P_TOP])
        best_v = sb("best_v", [P, P_TOP])
        best_i = sb("best_i", [P, P_TOP], u32)
        best_ab = sb("best_ab", [P, 2, P_TOP], u32)
        onehot = sb("onehot", [P, 2, P_TOP, P_TOP])
        e12 = sb("e12", [P, 2, P_TOP])
        lead = sb("lead", [P, 2, P_TOP])
        expo = sb("expo", [P, 2, P_TOP])
        expo_sum = sb("expo_sum", [P, 2])
        gates = sb("gates", [P, TILES, PICKS])
        eidx = sb("eidx", [P, TILES, PICKS], u32)
        idx_now = sb("idx_now", [P, 2, RING], u32)
        hb = sb("hb", [P, RING])
        ge = sb("ge", [P, RING])
        act_v = sb("act_v", [P, RING])
        diag = sb("diag", [P, 2 * BATCH, P])
        ss = sb("ss", [P, len(NORMS)])
        root = sb("root", [P, len(NORMS)])
        rstd = sb("rstd", [P, len(NORMS)])

        ring_flat = ring[:, :, :].rearrange("p r c -> p (r c)")
        at = [0]

        def in_ring(*dims):
            n = int(np.prod(dims))
            v = ring_flat[:, at[0]:at[0] + n]
            at[0] += n
            names = "abcd"[:len(dims)]
            sizes = {names[i]: dims[i] for i in range(len(dims) - 1)}
            return v if len(dims) == 1 else v.rearrange(f"p ({' '.join(names)}) -> p {' '.join(names)}", **sizes)

        w_sb = in_ring(KD, C_END)
        at[0] = 0
        logit = in_ring(A_HEADS * SEQ)
        p_t = in_ring(2, A_HEADS * P)
        o_t = in_ring(A_HEADS * P)
        rel = in_ring(I_HEADS * SEQ)
        relw = in_ring(I_HEADS * SEQ)
        s_t = in_ring(R_HEADS, 3 * P)
        ql_t = in_ring(A_HEADS * SEQ)
        b_tok = in_ring(TILES, R_HEADS * R_D)
        assert at[0] <= KD * C_END
        at[0] = KD * C_END
        qa_t = in_ring(4, SEQ)
        qi_t = in_ring(2, SEQ)
        ki_t = in_ring(SEQ)
        rqk = in_ring(2, 2, 2, SEQ)
        rv = in_ring(TILES, R_HEADS * R_D)
        rg = in_ring(TILES, R_HEADS * R_D)
        ukt_sb = in_ring(4, LATENT)
        uvw_sb = in_ring(A_HEADS * A_DIM)
        c_tok = in_ring(TILES, LATENT)
        c_t = in_ring(SEQ)
        wi = in_ring(TILES, I_HEADS)
        rot_sb = in_ring(2, SEQ)
        score = in_ring(TILES, SEQ)
        assert at[0] <= RING * 2 * D, at[0]
        h_t2 = conv_buf[:, 0:KD * SEQ].rearrange("p (k c) -> p k c", k=KD)
        mix_t = conv_buf[:, 0:TILES * KD * P].rearrange("p (t k c) -> p t k c", t=TILES, k=KD)
        z_flat = diag[:, :, :].rearrange("p k c -> p (k c)")
        rot_tmp = onehot[:, :, :, :].rearrange("p a b c -> p (a b c)")
        rot_tm2 = z_flat[:, 0:2 * SEQ]
        kvg = z_flat[:, 2 * SEQ:2 * SEQ + LATENT]
        ckv_raw = z_flat[:, 3 * SEQ:3 * SEQ + TILES * LATENT].rearrange("p (t c) -> p t c", t=TILES)
        decay_sb = wbuf[:, :, :, :].rearrange("p a k c -> p (a k c)")[:, 0:R_HEADS * 3 * P] \
            .rearrange("p (h c) -> p h c", h=R_HEADS)
        small = h_t[:, :, :].rearrange("p k c -> p (k c)")
        mask = small[:, 0:TILES * SEQ].rearrange("p (t c) -> p t c", t=TILES)
        taken = small[:, TILES * SEQ:TILES * SEQ + SEQ]
        n0 = (TILES + 1) * SEQ
        best8 = small[:, n0:n0 + 8]
        row_max = small[:, n0 + 8:n0 + 16]
        row_sum = small[:, n0 + 16:n0 + 24]
        row_inv = small[:, n0 + 24:n0 + 32]
        gn_stat = small[:, n0 + 32:n0 + 32 + 48].rearrange("p (g s) -> p g s", s=6)
        gn_mv = small[:, n0 + 80:n0 + 96].rearrange("p (g s) -> p g s", s=2)
        gn_root = small[:, n0 + 96:n0 + 104]
        gn_rstd = small[:, n0 + 104:n0 + 112]
        c_ss = small[:, n0 + 112:n0 + 114]
        c_root = small[:, n0 + 114:n0 + 116]
        c_rstd = small[:, n0 + 116:n0 + 118]

        acc = ctx.enter_context(nc.psum_tensor("acc", [P, HALF], f32))
        ps_s = ctx.enter_context(nc.psum_tensor("ps_s", [P, 2, 512], f32))
        ps_q = ps_s[:, :, 2 * P:4 * P]
        pm = ctx.enter_context(nc.psum_tensor("pm", [P, 4 * 512], f32))

        x_loaded = [sem(f"x_loaded{t}") for t in range(TILES)]
        w_in_loaded = [sem(f"w_in_loaded{i}") for i in range(len(W_PARTS))]
        rot_loaded, uk_loaded, small_loaded, decay_loaded = sem("rot_loaded"), sem("uk_loaded"), sem("small_loaded"), sem("decay_loaded")
        const_ready = sem("const_ready")
        gain_loaded = [sem(f"gain_loaded{i}") for i in range(2)]
        norm_root, h_ready, h_t_ps, h_t_ready = sem("norm_root"), sem("h_ready"), sem("h_t_ps"), sem("h_t_ready")
        x_ready = sem("x_ready")
        proj_ps = sem("proj_ps")
        proj_read = [sem(f"proj_read{b}") for b in range(4)]
        ckv_root, c_ready, c_t_ps, c_t_ready = sem("ckv_root"), sem("c_ready"), sem("c_t_ps"), sem("c_t_ready")
        idx_ps, rel_ready, score_ready, causal_ready = sem("idx_ps"), sem("rel_ready"), sem("score_ready"), sem("causal_ready")
        taken_ready, mask_ready = sem("taken_ready"), sem("mask_ready")
        rot_ready = sem("rot_ready")
        rg_sig = sem("rg_sig")
        ret_s_ps, ret_s_ready, ret_ps = sem("ret_s_ps"), sem("ret_s_ready"), sem("ret_ps")
        gn_var, gn_rooted, b_ready, b_t_ps, b_t_ready = sem("gn_var"), sem("gn_rooted"), sem("b_ready"), sem("b_t_ps"), sem("b_t_ready")
        ql_ps, ql_ready = sem("ql_ps"), sem("ql_ready")
        logit_ps, logit_ready, expo_ready, prob_ready = sem("logit_ps"), sem("logit_ready"), sem("attn_exp"), sem("prob_ready")
        p_t_ps, p_t_ready, o_ps, o_ready, a_ps, a_ready = (sem(n) for n in ("p_t_ps", "p_t_ready", "o_ps", "o_ready", "a_ps", "a_ready"))
        wo_ps, wo_read = sem("wo_ps"), sem("wo_read")
        w_loaded = [sem(f"w_loaded{i}") for i in range(WBUF)]
        q_ps, q_t_ready, s_ps, s_read, topk_on = sem("q_ps"), sem("q_t_ready"), sem("s_ps"), sem("s_read"), sem("topk_on")
        lead_ready, gate_exp, picks_ready = sem("lead_ready"), sem("gate_exp"), sem("picks_ready")
        gathered = [sem(f"gathered{r}") for r in range(RING)]
        idx_copied, may_gather = sem("idx_copied"), sem("may_gather")
        dots_ready, act_ready, diag_ready, v_added, v_multiplied = (sem(n) for n in ("dots_ready", "act_ready", "diag_ready", "v_added", "v_multiplied"))
        acc_closed = sem("acc_closed")
        pw_ps, sig_ready, glu_ready = sem("pw_ps"), sem("sig_ready"), sem("glu_ready")
        y_ready, mu_ps, yc_ready, ysq_ready, var_ps, root_ready, u_ready, zsig_ready, z_ready = (
            sem(n) for n in ("y_ready", "mu_ps", "yc_ready", "ysq_ready", "var_ps", "root_ready", "u_ready", "zsig_ready", "z_ready"))
        w2_ps = sem("w2_ps")
        stored = sem("stored")

        block = ctx.enter_context(nc.Block())

        PROJ = ([("ckv", t, 0) for t in range(TILES)] + [("qi", i, 0) for i in range(2)] + [("ki", 0, 0)]
                + [("qa", i, 1) for i in range(4)] + [("rot", i, 2 + i // 2) for i in range(4)]
                + [("rv", t, 4) for t in range(TILES)] + [("rg", t, 5) for t in range(TILES)])

        def job_of(kind, i=0):
            return next(n for n, (k, j, _) in enumerate(PROJ) if (k, j) == (kind, i))

        @block.sync
        def _(sp):
            for t in range(TILES):
                sp.dma_start(x_tok[:, t, :], x[t * P:(t + 1) * P, :]).then_inc(x_loaded[t], 16)
            sp.dma_start(gain[:, 0, :], gains[0:1, :].broadcast_to([P, D])).then_inc(gain_loaded[0], 16)
            sp.dma_start(gain[:, 1, :], gains[0:1, :].broadcast_to([P, D])).then_inc(gain_loaded[1], 16)
            for i, (a, b) in enumerate(W_PARTS):
                sp.dma_start(w_sb[:, :, a:b], w_in_v[:, :, a:b]).then_inc(w_in_loaded[i], 16)
                if i == 0:
                    sp.dma_start(kvg, kv_norm.broadcast_to([P, LATENT])).then_inc(uk_loaded, 16)
                    sp.dma_start(ukt_sb, uk_t).then_inc(uk_loaded, 16)
                    sp.dma_start(uvw_sb, uv_w).then_inc(uk_loaded, 16)
                    sp.dma_start(rot_sb, rot).then_inc(rot_loaded, 16)
                    sp.dma_start(decay_sb, decay).then_inc(decay_loaded, 16)
            sp.dma_start(keys_sb[:, :, :, :], keys_t).then_inc(small_loaded, 16)
            sp.dma_start(chan_sb[:, :], chan).then_inc(small_loaded, 16)
            sp.dma_start(b2_row[:, :], b2).then_inc(small_loaded, 16)

            def load_gain(e):
                sp.wait_ge(h_ready, e - 1)
                sp.dma_start(gain[:, e % 2, :], gains[NORMS[e][0]:NORMS[e][0] + 1, :].broadcast_to([P, D])) \
                  .then_inc(gain_loaded[e % 2], 16)

            def multiplied(n):
                if n < W_PHASE[0]:
                    return wo_ps, TILES * (n + 1)
                for p, first in enumerate(W_PHASE):
                    if first <= n < first + P_HEADS:
                        return q_ps, p * P_HEADS + n - first + 1
                for t, first in enumerate(W_CONV):
                    if first <= n < first + KD:
                        return pw_ps, t * KD + n - first + 1
                    if first + KD <= n < first + KD + 4:
                        return w2_ps, t * 4 + n - first - KD + 1

            def load_chunks(view, first, count):
                for c in range(count):
                    n = first + c
                    if n >= WBUF:
                        sp.wait_ge(*multiplied(n - WBUF))
                    else:
                        sp.wait_ge(ret_s_ready, 1)
                    sp.dma_start(wbuf[:, n % WBUF, :, :], view[:, :, c * WCOLS:(c + 1) * WCOLS]) \
                      .then_inc(w_loaded[n % WBUF], 16)

            def load_conv(t):
                load_chunks(w1_v, W_CONV[t], KD)
                load_chunks(w2_v, W_CONV[t] + KD, 4)

            load_gain(2)
            load_gain(3)
            load_chunks(w_o_v, W_O, 4)
            load_chunks(wq_v[0], W_PHASE[0], P_HEADS)
            load_gain(4)
            load_chunks(wq_v[0], W_PHASE[1], P_HEADS)
            load_gain(5)
            load_conv(0)
            load_gain(6)
            load_chunks(wq_v[1], W_PHASE[2], P_HEADS)
            load_gain(7)
            load_conv(1)
            load_gain(8)
            load_chunks(wq_v[1], W_PHASE[3], P_HEADS)
            load_gain(9)
            for t in range(TILES):
                sp.wait_ge(h_ready, FIN + t + 1)
                sp.dma_start(out[t * P:(t + 1) * P, :], h_tok[:, t, :]).then_inc(stored, 16)
            sp.wait_ge(stored, 16 * TILES)

        @block.gpsimd
        def _(pool):
            pool.memset(ident[:, :], 1.0)
            pool.memset(zeros[:, :], 0.0)
            pool.memset(mean_w[:, :], 1.0 / D)
            pool.memset(ones_row[:, :], 1.0)
            pool.memset(eps[:, :], EPS)
            pool.iota(iota16[:, :], [[1, P_TOP]], base=0, channel_multiplier=0,
                      allow_small_or_imprecise_dtypes=True).then_inc(const_ready, 1)
            pool.wait_ge(const_ready, 1)
            pool.affine_select(out=ident[:, :], in_=ident[:, :], compare_op=ALU.is_equal, fill=0.0, base=0,
                               pattern=[[-1, P]], channel_multiplier=1).then_inc(const_ready, 1)
            for t in range(TILES):
                s = P * (t + 1)
                for src, ready, fill, done in ((score, score_ready, MASKED, causal_ready), (mask, taken_ready, OFF, mask_ready)):
                    pool.wait_ge(ready, t + 1)
                    pool.affine_select(out=src[:, t, 0:s], in_=src[:, t, 0:s], compare_op=ALU.is_ge, fill=fill,
                                       base=P * t, pattern=[[-1, s]], channel_multiplier=1).then_inc(done, 1)

            def gathers(p):
                layer, t = p // 2, p % 2
                rounds = PICKS // RING
                with pool.Fori(0, rounds // 2) as i:
                    for half in range(2):
                        r0 = p * rounds + half
                        pool.wait_ge(picks_ready, i * 2 + (r0 + 1))
                        pool.wait_ge(v_added, i * (2 * RING) + (r0 * RING + 1))
                        pool.sem_inc(may_gather, 1)
                        pool.tensor_copy(idx_now[:, half, :], eidx[:, t, ds(i * (2 * RING) + half * RING, RING)]) \
                            .then_inc(idx_copied, 1)
                        pool.wait_ge(idx_copied, i * 2 + (r0 + 1))
                        for r in range(RING):
                            freed = r0 * RING + r + 1
                            pool.wait_ge(v_added, i * (2 * RING) + freed)
                            pool.wait_ge(v_multiplied, i * (2 * RING) + freed)
                            pool.sem_inc(may_gather, 1)
                            pool.indirect_dma_start(ring[:, r, :], None, table[layer],
                                                    bass.IndirectOffsetOnAxis(idx_now[:, half, r:r + 1], 0)) \
                                .then_inc(gathered[r], 16)

            pool.wait_ge(x_ready, 2)
            for p in range(2 * LAYERS):
                gathers(p)

        @block.scalar
        def _(act):
            def norm(e):
                t = NORMS[e][1]
                if e < 2:
                    act.wait_ge(x_loaded[t], 16)
                else:
                    act.wait_ge(x_ready, X_OF_NORM[e])
                act.activation(h_tok[:, t, :], x_tok[:, t, :], ACT.Square, accum_out=ss[:, e:e + 1])
                act.drain()
                act.activation(root[:, e:e + 1], ss[:, e:e + 1], ACT.Sqrt, bias=eps[:, :], scale=1.0 / D).then_inc(norm_root, 1)

            def keep_h_t(e, dst, half):
                act.wait_ge(h_t_ps, e + 1)
                act.copy(dst, pm[:, half * 1024:half * 1024 + 1024].rearrange("p (k c) -> p k c", k=KD)).then_inc(h_t_ready, 1)

            act.wait_ge(const_ready, 2)
            norm(0)
            norm(1)
            keep_h_t(0, h_t2[:, :, 0:P], 0)
            keep_h_t(1, h_t2[:, :, P:SEQ], 1)

            def read(kind, i=0):
                n = job_of(kind, i)
                act.wait_ge(proj_ps, n + 1)
                return pm[:, (n % 4) * 512:(n % 4) * 512 + 512], proj_read[n % 4]

            for t in range(TILES):
                ps, done = read("ckv", t)
                act.copy(ckv_raw[:, t, :], ps[:, 0:LATENT])
                act.mul(wi[:, t, :].rearrange("p (a b) -> p a b", a=4),
                        ps[:, LATENT:LATENT + I_HEADS].rearrange("p (b a) -> p a b", a=4), I_HEADS ** -0.5).then_inc(done, 1)
                act.drain()
                act.activation(c_tok[:, t, :], ckv_raw[:, t, :], ACT.Square, accum_out=c_ss[:, t:t + 1])
                act.drain()
                act.activation(c_root[:, t:t + 1], c_ss[:, t:t + 1], ACT.Sqrt, bias=eps[:, :], scale=1.0 / LATENT).then_inc(ckv_root, 1)
            for kind, n, dst in (("qi", 2, qi_t), ("ki", 1, None), ("qa", 4, qa_t)):
                for i in range(n):
                    ps, done = read(kind, i)
                    act.copy(ki_t if dst is None else dst[:, i, :], ps[:, 0:SEQ]).then_inc(done, 1)
            for t in range(TILES):
                ps, done = read("rv", t)
                act.copy(rv[:, t, :], ps[:, :]).then_inc(done, 1)
            for t in range(TILES):
                n = job_of("rg", t)
                act.wait_ge(proj_ps, n + 1)
                act.activation(rg[:, t, :], pm[:, (n % 4) * 512:(n % 4) * 512 + 512], ACT.Sigmoid).then_inc(rg_sig, 1)
            act.wait_ge(c_t_ps, 2)
            act.copy(c_t, ps_s[:, 0, 0:SEQ]).then_inc(c_t_ready, 1)
            for t in range(TILES):
                s = P * (t + 1)
                act.wait_ge(idx_ps, t + 1)
                if t:
                    act.wait_ge(score_ready, t)
                act.activation(rel[:, 0:I_HEADS * s].rearrange("p (a c) -> p a c", a=4),
                               pm[:, :].rearrange("p (a c) -> p a c", a=4)[:, :, 0:2 * s], ACT.Relu).then_inc(rel_ready, 1)
            act.wait_ge(gn_var, 1)
            act.activation(gn_root, gn_mv[:, :, 1:2].rearrange("p g s -> p (g s)"), ACT.Sqrt, bias=eps[:, :]).then_inc(gn_rooted, 1)
            act.wait_ge(b_t_ps, 1)
            act.copy(mix_t[:, :, 4:8, :], pm[:, 0:1024].rearrange("p (t k c) -> p t k c", t=2, k=4)).then_inc(b_t_ready, 1)
            act.wait_ge(ql_ps, 1)
            act.copy(ql_t, pm[:, :]).then_inc(ql_ready, 1)
            for t in range(TILES):
                n = A_HEADS * P * (t + 1)
                act.wait_ge(logit_ready, t + 1)
                act.activation(logit[:, 0:n], logit[:, 0:n], ACT.Exp).then_inc(expo_ready, 1)
                act.wait_ge(p_t_ps, t + 1)
                act.copy(p_t[:, 0:t + 1, :], pm[:, 0:n].rearrange("p (s c) -> p s c", s=t + 1)).then_inc(p_t_ready, 1)
                act.wait_ge(o_ps, t + 1)
                act.copy(o_t, pm[:, 0:1024]).then_inc(o_ready, 1)
                act.wait_ge(a_ps, t + 1)
                act.copy(mix_t[:, t, 0:4, :], pm[:, 1024:1536].rearrange("p (k c) -> p k c", k=4)).then_inc(a_ready, 1)

            def keep_input(e):
                keep_h_t(e, h_t[:, :, :], e % 2 if e < 4 else 0)

            def keep_queries(p, i):
                for b in range(2):
                    u = p * P_HEADS + b
                    act.wait_ge(q_ps, i * 2 + (u + 1))
                    act.copy(q_t[:, b, :], ps_q[:, b, :]).then_inc(q_t_ready, 1)

            def gate_exps(p, i):
                for b in range(2):
                    act.wait_ge(lead_ready, i * 2 + (p * P_HEADS + b + 1))
                    act.activation(expo[:, b, :], lead[:, b, :], ACT.Exp, accum_out=expo_sum[:, b:b + 1]).then_inc(gate_exp, 1)

            def expert_round(p, i):
                t = p % 2
                for b in range(RING // BATCH):
                    n0 = p * PICKS + b * BATCH
                    c = slice(b * BATCH, (b + 1) * BATCH)
                    act.wait_ge(dots_ready, i * RING + (n0 + BATCH))
                    act.activation(ge[:, c], hb[:, c], ACT.Gelu)
                    act.drain()
                    for j in range(BATCH):
                        r = b * BATCH + j
                        last = act.activation(act_v[:, r:r + 1], ge[:, r:r + 1], ACT.Copy,
                                              scale=gates[:, t, ds(i * RING + r, 1)])
                    last.then_inc(act_ready, BATCH)
                    act.drain()
                    act.wait_ge(v_multiplied, i * RING + (RING + n0 - BATCH))
                    for j in range(BATCH):
                        r = b * BATCH + j
                        act.activation(diag[:, (b % 2) * BATCH + j, :], ident[:, :], ACT.Copy,
                                       scale=act_v[:, r:r + 1]).then_inc(diag_ready, 1)
                act.drain()

            def gates_of_glu(t, i):
                for c in range(4):
                    n = t * KD + c
                    act.wait_ge(pw_ps, i * 4 + (n + 1))
                    act.wait_ge(glu_ready, i * 4 + (n + 1))
                    act.activation(gate_sig[:, c, :], pm[:, c * 512 + P:c * 512 + 2 * P], ACT.Sigmoid,
                                   bias=chan_sb[:, ds(i * 4 + (CP_BG + c), 1)]).then_inc(sig_ready, 1)

            def conv_norm(t):
                act.wait_ge(yc_ready, t + 1)
                act.activation(z_t[:, :, :], y_t[:, :, :], ACT.Square).then_inc(ysq_ready, 1)
                act.wait_ge(var_ps, t + 1)
                act.activation(rstd_y[:, :], pm[:, P:2 * P], ACT.Sqrt, bias=eps[:, :]).then_inc(root_ready, 1)
                act.wait_ge(u_ready, t + 1)
                act.activation(z_t[:, :, :], y_t[:, :, :], ACT.Sigmoid).then_inc(zsig_ready, 1)

            norm(2)
            keep_input(2)
            keep_queries(0, 0)
            gate_exps(0, 0)
            keep_queries(0, 1)
            gate_exps(0, 1)
            keep_queries(0, 2)
            expert_round(0, 0)
            gate_exps(0, 2)
            keep_queries(0, 3)
            expert_round(0, 1)
            gate_exps(0, 3)
            norm(3)
            expert_round(0, 2)
            keep_input(3)
            keep_queries(1, 0)
            with act.Fori(0, 3) as i:
                expert_round(0, i + 3)
                gate_exps(1, i)
                keep_queries(1, i + 1)
            expert_round(0, 6)
            gate_exps(1, 3)
            expert_round(0, 7)
            for p in (1, 2):
                t = p - 1
                norm(2 * p + 2)
                keep_input(2 * p + 2)
                gates_of_glu(t, 0)
                expert_round(p, 0)
                gates_of_glu(t, 1)
                expert_round(p, 1)
                expert_round(p, 2)
                conv_norm(t)
                expert_round(p, 3)
                norm(2 * p + 3)
                keep_input(2 * p + 3)
                keep_queries(p + 1, 0)
                with act.Fori(0, 3) as i:
                    expert_round(p, i + 4)
                    gate_exps(p + 1, i)
                    keep_queries(p + 1, i + 1)
                expert_round(p, 7)
                gate_exps(p + 1, 3)
            norm(8)
            with act.Fori(0, 8) as i:
                expert_round(3, i)
            norm(9)

        @block.vector
        def _(dve):
            def norm(e):
                t = NORMS[e][1]
                dve.wait_ge(norm_root, e + 1)
                dve.reciprocal(rstd[:, e:e + 1], root[:, e:e + 1])
                dve.drain()
                dve.wait_ge(gain_loaded[e % 2], 16 * (e // 2 + 1))
                dve.scalar_tensor_tensor(out=h_tok[:, t, :], in0=x_tok[:, t, :], scalar=rstd[:, e:e + 1],
                                         in1=gain[:, e % 2, :], op0=ALU.mult, op1=ALU.mult).then_inc(h_ready, 1)

            dve.sem_inc(s_read, 2)
            dve.sem_inc(glu_ready, 4)
            dve.sem_inc(v_added, RING)
            norm(0)
            norm(1)
            dve.wait_ge(uk_loaded, 48)
            for t in range(TILES):
                dve.wait_ge(ckv_root, t + 1)
                dve.reciprocal(c_rstd[:, t:t + 1], c_root[:, t:t + 1])
                dve.drain()
                dve.scalar_tensor_tensor(out=c_tok[:, t, :], in0=ckv_raw[:, t, :], scalar=c_rstd[:, t:t + 1],
                                         in1=kvg, op0=ALU.mult, op1=ALU.mult).then_inc(c_ready, 1)
            dve.wait_ge(rot_loaded, 16)
            for i in range(4):
                n = job_of("rot", i)
                dve.wait_ge(proj_ps, n + 1)
                ps = pm[:, (n % 4) * 512:(n % 4) * 512 + 512].rearrange("p (a c) -> p a c", a=2)
                for a in range(2):
                    dve.tensor_tensor(rot_tmp[:, a * SEQ:(a + 1) * SEQ], ps[:, a, :], rot_sb[:, 0, :], ALU.mult)
                    last = dve.tensor_tensor(rot_tm2[:, a * SEQ:(a + 1) * SEQ], ps[:, 1 - a, :], rot_sb[:, 1, :], ALU.mult)
                last.then_inc(proj_read[n % 4], 1)
                dve.drain()
                dve.tensor_tensor(rqk[:, i // 2, i % 2, 0, :], rot_tmp[:, 0:SEQ], rot_tm2[:, 0:SEQ], ALU.subtract)
                dve.tensor_tensor(rqk[:, i // 2, i % 2, 1, :], rot_tmp[:, SEQ:2 * SEQ], rot_tm2[:, SEQ:2 * SEQ],
                                  ALU.add).then_inc(rot_ready, 1)
                dve.drain()
            for t in range(TILES):
                n = job_of("rg", t)
                dve.wait_ge(rg_sig, t + 1)
                dve.tensor_tensor(rg[:, t, :], pm[:, (n % 4) * 512:(n % 4) * 512 + 512], rg[:, t, :], ALU.mult) \
                    .then_inc(proj_read[n % 4], 1)
            for t in range(TILES):
                s = P * (t + 1)
                dve.wait_ge(rel_ready, t + 1)
                dve.tensor_tensor(relw[:, 0:I_HEADS * s].rearrange("p (h s) -> p h s", h=I_HEADS),
                                  rel[:, 0:I_HEADS * s].rearrange("p (h s) -> p h s", h=I_HEADS),
                                  wi[:, t, :].unsqueeze(2).broadcast_to([P, I_HEADS, s]), ALU.mult)
                dve.drain()
                dve.tensor_reduce(score[:, t, 0:s], relw[:, 0:I_HEADS * s].rearrange("p (h s) -> p s h", h=I_HEADS),
                                  AX.X, ALU.add).then_inc(score_ready, 1)
                dve.drain()
            for t in range(TILES):
                s = P * (t + 1)
                dve.wait_ge(causal_ready, t + 1)
                for _ in range(TOPK // 8):
                    dve.max(best8, score[:, t, 0:s])
                    dve.drain()
                    dve.match_replace(score[:, t, 0:s], best8, score[:, t, 0:s], TAKEN)
                    dve.drain()
                dve.tensor_scalar(mask[:, t, 0:s], score[:, t, 0:s], TAKEN, OFF, ALU.not_equal, ALU.mult).then_inc(taken_ready, 1)
            dve.wait_ge(ret_s_ps, 1)
            dve.wait_ge(decay_loaded, 16)
            dve.tensor_tensor(s_t, pm[:, :].rearrange("p (h c) -> p h c", h=R_HEADS)[:, :, 0:3 * P], decay_sb,
                              ALU.mult).then_inc(ret_s_ready, 1)
            dve.wait_ge(ret_ps, 1)
            for g in range(TILES * R_HEADS):
                dve.bn_stats(gn_stat[:, g, :], pm[:, g * R_D:(g + 1) * R_D])
            dve.drain()
            for g in range(TILES * R_HEADS):
                last = dve.bn_aggr(gn_mv[:, g, :], gn_stat[:, g, :])
            last.then_inc(gn_var, 1)
            dve.wait_ge(gn_rooted, 1)
            dve.reciprocal(gn_rstd, gn_root)
            dve.drain()
            for g in range(TILES * R_HEADS):
                t, h = g // R_HEADS, g % R_HEADS
                dve.tensor_scalar(b_tok[:, t, h * R_D:(h + 1) * R_D], pm[:, g * R_D:(g + 1) * R_D],
                                  gn_mv[:, g, 0:1], gn_rstd[:, g:g + 1], ALU.subtract, ALU.mult)
            dve.drain()
            dve.tensor_tensor(b_tok, b_tok, rg, ALU.mult).then_inc(b_ready, 1)
            for t in range(TILES):
                s = P * (t + 1)
                n = A_HEADS * s
                lg = logit[:, 0:n].rearrange("p (h s) -> p h s", h=A_HEADS)
                dve.wait_ge(logit_ps, t + 1)
                dve.wait_ge(mask_ready, t + 1)
                dve.scalar_tensor_tensor(out=lg, in0=pm[:, 0:n].rearrange("p (h s) -> p h s", h=A_HEADS),
                                         scalar=A_DIM ** -0.5, in1=mask[:, t, 0:s].unsqueeze(1).broadcast_to([P, A_HEADS, s]),
                                         op0=ALU.mult, op1=ALU.add)
                dve.drain()
                dve.tensor_reduce(row_max, lg, AX.X, ALU.max)
                dve.drain()
                dve.tensor_tensor(lg, lg, row_max.unsqueeze(2).broadcast_to([P, A_HEADS, s]), ALU.subtract).then_inc(logit_ready, 1)
                dve.wait_ge(expo_ready, t + 1)
                dve.tensor_reduce(row_sum, lg, AX.X, ALU.add)
                dve.drain()
                dve.reciprocal(row_inv, row_sum)
                dve.drain()
                dve.tensor_tensor(lg, lg, row_inv.unsqueeze(2).broadcast_to([P, A_HEADS, s]), ALU.mult).then_inc(prob_ready, 1)
                dve.drain()
            for c in range(4):
                for t in range(TILES):
                    n = 2 * c + t
                    dve.wait_ge(wo_ps, n + 1)
                    xs = x_tok[:, t, c * WCOLS:(c + 1) * WCOLS]
                    dve.tensor_tensor(xs, xs, pm[:, (n % 4) * 512:(n % 4) * 512 + WCOLS], ALU.add).then_inc(wo_read, 1)
                    if c == 3:
                        dve.drain().then_inc(x_ready, 1)

            def topk(p, i, b):
                t, u = p % 2, p * P_HEADS + b
                dve.wait_ge(s_ps, i * 2 + (u + 1))
                dve.sem_inc(topk_on, 1)
                side = [ps_s[:, b, j * P:(j + 1) * P] for j in range(2)]
                for j in range(2):
                    dve.max(top_v[:, j, 0:8], side[j])
                dve.drain()
                for j in range(2):
                    dve.max_index(top_i[:, j, 0:8], top_v[:, j, 0:8], side[j])
                    last = dve.match_replace(rest[:, j, :], top_v[:, j, 0:8], side[j], LOWEST)
                last.then_inc(s_read, 1)
                dve.drain()
                for j in range(2):
                    dve.max(top_v[:, j, 8:16], rest[:, j, :])
                dve.drain()
                for j in range(2):
                    dve.max_index(top_i[:, j, 8:16], top_v[:, j, 8:16], rest[:, j, :])
                dve.tensor_tensor(cand[:, :, :], top_v[:, 0, :].unsqueeze(2).broadcast_to([P, P_TOP, P_TOP]),
                                  top_v[:, 1, :].unsqueeze(1).broadcast_to([P, P_TOP, P_TOP]), ALU.add)
                dve.drain()
                flat, flat2 = (v[:, :, :].rearrange("p a b -> p (a b)") for v in (cand, cand2))
                dve.max(best_v[:, 0:8], flat)
                dve.drain()
                dve.max_index(best_i[:, 0:8], best_v[:, 0:8], flat)
                dve.match_replace(flat2, best_v[:, 0:8], flat, LOWEST)
                dve.drain()
                dve.max(best_v[:, 8:16], flat2)
                dve.drain()
                dve.max_index(best_i[:, 8:16], best_v[:, 8:16], flat2)
                dve.tensor_scalar(lead[:, b, :], best_v[:, :], best_v[:, 0:1], None, ALU.subtract).then_inc(lead_ready, 1)
                dve.drain()
                dve.tensor_scalar(best_ab[:, 0, :], best_i[:, :], 4, None, ALU.logical_shift_right)
                dve.tensor_scalar(best_ab[:, 1, :], best_i[:, :], P_TOP - 1, None, ALU.bitwise_and)
                dve.drain()
                dve.tensor_tensor(onehot[:, :, :, :], best_ab[:, :, :].unsqueeze(3).broadcast_to([P, 2, P_TOP, P_TOP]),
                                  iota16[:, :].unsqueeze(1).unsqueeze(1).broadcast_to([P, 2, P_TOP, P_TOP]), ALU.is_equal)
                dve.drain()
                dve.tensor_tensor(onehot[:, :, :, :], onehot[:, :, :, :],
                                  top_i[:, :, :].unsqueeze(2).broadcast_to([P, 2, P_TOP, P_TOP]), ALU.mult)
                dve.drain()
                dve.tensor_reduce(e12[:, :, :], onehot[:, :, :, :], AX.X, ALU.add)
                dve.drain()
                dve.scalar_tensor_tensor(out=eidx[:, t, ds(i * (2 * P_TOP) + b * P_TOP, P_TOP)], in0=e12[:, 0, :],
                                         scalar=float(P), in1=e12[:, 1, :], op0=ALU.mult, op1=ALU.add)
                dve.drain()

            def heads(p, i):
                for b in range(2):
                    topk(p, i, b)
                for b in range(2):
                    dve.wait_ge(gate_exp, i * 2 + (p * P_HEADS + b + 1))
                    dve.reciprocal(expo_sum[:, b:b + 1], expo_sum[:, b:b + 1])
                    dve.drain()
                    dve.tensor_scalar(gates[:, p % 2, ds(i * (2 * P_TOP) + b * P_TOP, P_TOP)], expo[:, b, :],
                                      expo_sum[:, b:b + 1], None, ALU.mult).then_inc(picks_ready, 1)
                dve.drain()

            def expert_round(p, i):
                t = p % 2
                rounds = PICKS // RING
                xs = x_tok[:, t, 0:HALF]

                def dots(b):
                    for j in range(BATCH):
                        r = b * BATCH + j
                        dve.wait_ge(gathered[r], i * 16 + 16 * (p * rounds + 1))
                        dve.scalar_tensor_tensor(out=ring[:, r, 0:D], in0=ring[:, r, 0:D], scalar=1.0, in1=h_tok[:, t, :],
                                                 op0=ALU.mult, op1=ALU.mult, accum_out=hb[:, r:r + 1]).then_inc(dots_ready, 1)

                def add_v(b):
                    n0 = p * PICKS + b * BATCH
                    dve.wait_ge(act_ready, i * RING + (n0 + BATCH))
                    for j in range(BATCH):
                        r = b * BATCH + j
                        dve.scalar_tensor_tensor(out=xs, in0=ring[:, r, D:D + HALF], scalar=act_v[:, r:r + 1], in1=xs,
                                                 op0=ALU.mult, op1=ALU.add).then_inc(v_added, 1)
                        dve.drain()

                dots(0)
                for b in range(1, RING // BATCH):
                    dots(b)
                    add_v(b - 1)
                add_v(RING // BATCH - 1)

            def close_sum(p):
                dve.wait_ge(acc_closed, p + 1)
                dve.tensor_copy(x_tok[:, p % 2, HALF:D], acc[:, :]).then_inc(x_ready, 1)

            def glu_history(t):
                if t:
                    dve.tensor_copy(glu[:, :, 0:HIST], glu[:, :, P:P + HIST])
                    dve.drain()
                else:
                    dve.wait_ge(small_loaded, 48)
                    dve.memset(glu[:, :, 0:HIST], 0.0)

            def conv_quad(t, i):
                for c in range(4):
                    n = t * KD + c
                    dve.wait_ge(sig_ready, i * 4 + (n + 1))
                    dve.scalar_tensor_tensor(out=glu[:, ds(i * 4 + c, 1), HIST:HIST + P].rearrange("p a c -> p (a c)"),
                                             in0=pm[:, c * 512:c * 512 + P],
                                             scalar=chan_sb[:, ds(i * 4 + (CP_BA + c), 1)],
                                             in1=gate_sig[:, c, :], op0=ALU.add, op1=ALU.mult).then_inc(glu_ready, 1)
                dve.drain()
                for w in range(TAPS):
                    for c in range(4):
                        src = glu[:, ds(i * 4 + c, 1), w:w + P].rearrange("p a c -> p (a c)")
                        dst = y_t[:, ds(i * 4 + c, 1), :].rearrange("p a c -> p (a c)")
                        tap = chan_sb[:, ds(i * (4 * TAPS) + (CP_DW + c * TAPS + w), 1)]
                        if w == 0:
                            dve.tensor_scalar(dst, src, tap, chan_sb[:, ds(i * 4 + (CP_DWB + c), 1)], ALU.mult, ALU.add)
                        else:
                            dve.scalar_tensor_tensor(out=dst, in0=src, scalar=tap, in1=dst, op0=ALU.mult, op1=ALU.add)
                    if w < TAPS - 1:
                        dve.drain()
                dve.drain().then_inc(y_ready, 1)

            def conv_norm(t):
                dve.wait_ge(mu_ps, t + 1)
                dve.tensor_tensor(y_t[:, :, :], y_t[:, :, :], pm[:, 0:P].unsqueeze(1).broadcast_to([P, KD, P]),
                                  ALU.subtract).then_inc(yc_ready, 1)
                dve.wait_ge(root_ready, t + 1)
                dve.reciprocal(rstd_y[:, :], rstd_y[:, :])
                dve.drain()
                dve.tensor_tensor(y_t[:, :, :], y_t[:, :, :], rstd_y[:, :].unsqueeze(1).broadcast_to([P, KD, P]), ALU.mult)
                dve.drain()
                for c in range(KD):
                    last = dve.tensor_scalar(y_t[:, c, :], y_t[:, c, :], chan_sb[:, CP_G + c:CP_G + c + 1],
                                             chan_sb[:, CP_B + c:CP_B + c + 1], ALU.mult, ALU.add)
                last.then_inc(u_ready, 1)
                dve.wait_ge(zsig_ready, t + 1)
                dve.tensor_tensor(z_t[:, :, :], z_t[:, :, :], y_t[:, :, :], ALU.mult).then_inc(z_ready, 1)

            def conv_out(t):
                for c in range(4):
                    n = 4 * t + c
                    dve.wait_ge(w2_ps, n + 1)
                    xs = x_tok[:, t, c * WCOLS:(c + 1) * WCOLS]
                    dve.tensor_tensor(xs, xs, pm[:, c * 512:c * 512 + WCOLS], ALU.add)
                dve.drain().then_inc(x_ready, 1)

            dve.wait_ge(const_ready, 2)
            norm(2)
            heads(0, 0)
            heads(0, 1)
            expert_round(0, 0)
            heads(0, 2)
            expert_round(0, 1)
            heads(0, 3)
            expert_round(0, 2)
            norm(3)
            with dve.Fori(0, 4) as i:
                expert_round(0, i + 3)
                heads(1, i)
            expert_round(0, 7)
            close_sum(0)
            for p in (1, 2):
                t = p - 1
                norm(2 * p + 2)
                glu_history(t)
                expert_round(p, 0)
                with dve.Fori(0, 2) as i:
                    conv_quad(t, i)
                    expert_round(p, i + 1)
                conv_norm(t)
                expert_round(p, 3)
                conv_out(t)
                norm(2 * p + 3)
                with dve.Fori(0, 3) as i:
                    expert_round(p, i + 4)
                    heads(p + 1, i)
                expert_round(p, 7)
                close_sum(p)
                heads(p + 1, 3)
            norm(8)
            with dve.Fori(0, 8) as i:
                expert_round(3, i)
            close_sum(3)
            norm(9)

        @block.tensor
        def _(pe):
            def transpose_h(e, half):
                t = NORMS[e][1]
                pe.wait_ge(h_ready, e + 1)
                for k in range(KD):
                    last = pe.transpose(pm[:, half * 1024 + k * P:half * 1024 + (k + 1) * P], h_tok[:, t, k * P:(k + 1) * P], ident[:, :])
                last.then_inc(h_t_ps, 1)

            def product(dst, lhs, rhs):
                for k in range(KD):
                    last = pe.matmul(dst, lhs(k), rhs(k), start=(k == 0), stop=(k == KD - 1))
                return last

            pe.sem_inc(v_multiplied, RING)
            pe.wait_ge(const_ready, 2)
            transpose_h(0, 0)
            transpose_h(1, 1)
            pe.wait_ge(h_t_ready, 2)
            for n, (kind, i, part) in enumerate(PROJ):
                pe.wait_ge(w_in_loaded[part], 16)
                if n >= 4:
                    pe.wait_ge(proj_read[n % 4], n // 4)
                ps = pm[:, (n % 4) * 512:(n % 4) * 512 + 512]
                if kind == "ckv":
                    tok = slice(i * P, (i + 1) * P)
                    product(ps[:, 0:LATENT], lambda k: h_t2[:, k, tok], lambda k: w_sb[:, k, C_CKV:C_CKV + LATENT])
                    last = product(ps[:, LATENT:LATENT + I_HEADS], lambda k: h_t2[:, k, tok], lambda k: w_sb[:, k, C_WI:C_WI + I_HEADS])
                elif kind == "qi":
                    last = product(ps[:, 0:SEQ], lambda k: w_sb[:, k, C_QI + i * P:C_QI + (i + 1) * P], lambda k: h_t2[:, k, :])
                elif kind == "ki":
                    for g in range(4):
                        last = product(ps[g * I_DIM:(g + 1) * I_DIM, 0:SEQ], lambda k: w_sb[:, k, C_KI:C_KI + I_DIM], lambda k: h_t2[:, k, :])
                elif kind == "qa":
                    last = product(ps[:, 0:SEQ], lambda k: w_sb[:, k, C_QA + i * P:C_QA + (i + 1) * P], lambda k: h_t2[:, k, :])
                elif kind == "rot":
                    c0 = (C_RQ, C_RK)[i // 2] + (i % 2) * 2 * R_D
                    for a in range(2):
                        last = product(ps[:, a * SEQ:(a + 1) * SEQ], lambda k: w_sb[:, k, c0 + a:c0 + a + 2 * R_D - 1:2], lambda k: h_t2[:, k, :])
                else:
                    tok = slice(i * P, (i + 1) * P)
                    c0 = C_RV if kind == "rv" else C_RG
                    last = product(ps[:, :], lambda k: h_t2[:, k, tok], lambda k: w_sb[:, k, c0:c0 + R_HEADS * R_D])
                last.then_inc(proj_ps, 1)
            for t in range(TILES):
                pe.wait_ge(c_ready, t + 1)
                pe.transpose(ps_s[:, 0, t * P:(t + 1) * P], c_tok[:, t, :], ident[:, :]).then_inc(c_t_ps, 1)
            for b in range(4):
                pe.wait_ge(proj_read[b], sum(1 for n in range(len(PROJ)) if n % 4 == b))
            for t in range(TILES):
                s = P * (t + 1)
                if t:
                    pe.wait_ge(rel_ready, t)
                for h in range(I_HEADS):
                    rows = slice((h % 4) * I_DIM, (h % 4 + 1) * I_DIM)
                    c0 = (h % 4) * 512 + (h // 4) * s
                    last = pe.matmul(pm[:, c0:c0 + s], qi_t[rows, h // 4, t * P:(t + 1) * P], ki_t[rows, 0:s], start=True, stop=True)
                last.then_inc(idx_ps, 1)
            pe.wait_ge(rel_ready, 2)
            pe.wait_ge(rot_ready, 4)
            for h in range(R_HEADS):
                rows = slice((h % 2) * 64, (h % 2) * 64 + 64)
                for n, (s, c) in enumerate(((0, 0), (1, 1), (0, 1))):
                    for a in range(2):
                        last = pe.matmul(pm[:, h * 512 + n * P:h * 512 + (n + 1) * P],
                                         rqk[rows, 1, h // 2, a, s * P:(s + 1) * P], rqk[rows, 0, h // 2, a, c * P:(c + 1) * P],
                                         start=(a == 0), stop=(a == 1))
            last.then_inc(ret_s_ps, 1)
            pe.wait_ge(ret_s_ready, 1)
            for t in range(TILES):
                for h in range(R_HEADS):
                    dst = pm[:, t * 512 + h * R_D:t * 512 + (h + 1) * R_D]
                    v = slice(h * R_D, (h + 1) * R_D)
                    if t == 0:
                        last = pe.matmul(dst, s_t[:, h, 0:P], rv[:, 0, v], start=True, stop=True)
                    else:
                        pe.matmul(dst, s_t[:, h, 2 * P:3 * P], rv[:, 0, v], start=True, stop=False)
                        last = pe.matmul(dst, s_t[:, h, P:2 * P], rv[:, 1, v], start=False, stop=True)
            last.then_inc(ret_ps, 1)
            pe.wait_ge(b_ready, 1)
            for t in range(TILES):
                for h in range(R_HEADS):
                    last = pe.transpose(pm[:, t * 512 + h * P:t * 512 + (h + 1) * P], b_tok[:, t, h * R_D:(h + 1) * R_D], ident[:, :])
            last.then_inc(b_t_ps, 1)
            pe.wait_ge(b_t_ready, 1)
            pe.wait_ge(uk_loaded, 48)

            def ql_at(h):
                return (h % 2) * 1024 + (h // 2) * SEQ

            for h in range(A_HEADS):
                rows = slice((h % 2) * A_DIM, (h % 2 + 1) * A_DIM)
                last = pe.matmul(pm[:, ql_at(h):ql_at(h) + SEQ], ukt_sb[rows, h // 2, :], qa_t[rows, h // 2, :], start=True, stop=True)
            last.then_inc(ql_ps, 1)
            pe.wait_ge(ql_ready, 1)
            pe.wait_ge(c_t_ready, 1)
            for t in range(TILES):
                s = P * (t + 1)
                if t:
                    pe.wait_ge(a_ready, t)
                for h in range(A_HEADS):
                    last = pe.matmul(pm[:, h * s:(h + 1) * s], ql_t[:, ql_at(h) + t * P:ql_at(h) + (t + 1) * P], c_t[:, 0:s], start=True, stop=True)
                last.then_inc(logit_ps, 1)
                pe.wait_ge(prob_ready, t + 1)
                for k in range(t + 1):
                    for h in range(A_HEADS):
                        last = pe.transpose(pm[:, (k * A_HEADS + h) * P:(k * A_HEADS + h + 1) * P],
                                            logit[:, h * s + k * P:h * s + (k + 1) * P], ident[:, :])
                last.then_inc(p_t_ps, 1)
                pe.wait_ge(p_t_ready, t + 1)
                for half in range(2):
                    for k in range(t + 1):
                        last = pe.matmul(pm[:, half * 512:(half + 1) * 512], c_tok[:, k, :], p_t[:, k, half * 512:(half + 1) * 512],
                                         start=(k == 0), stop=(k == t))
                last.then_inc(o_ps, 1)
                pe.wait_ge(o_ready, t + 1)
                for h in range(A_HEADS):
                    last = pe.matmul(pm[(h % 2) * A_DIM:(h % 2 + 1) * A_DIM, 1024 + (h // 2) * P:1024 + (h // 2 + 1) * P],
                                     uvw_sb[:, h * A_DIM:(h + 1) * A_DIM], o_t[:, h * P:(h + 1) * P], start=True, stop=True)
                last.then_inc(a_ps, 1)

            def chunk(n):
                pe.wait_ge(w_loaded[n % WBUF], 16 * (n // WBUF + 1))
                return wbuf[:, n % WBUF, :, :]

            pe.wait_ge(a_ready, 2)
            for c in range(4):
                w = chunk(W_O + c)
                for t in range(TILES):
                    n = 2 * c + t
                    if n >= 4:
                        pe.wait_ge(wo_read, n - 3)
                    last = product(pm[:, (n % 4) * 512:(n % 4) * 512 + WCOLS], lambda k: mix_t[:, t, k, :], lambda k: w[:, k, :])
                    last.then_inc(wo_ps, 1)

            def norm_h_t(e):
                transpose_h(e, e % 2 if e < 4 else 0)

            def await_h_t(e):
                pe.wait_ge(h_t_ready, e + 1)

            def heads_start(p):
                await_h_t((2, 3, 5, 7)[p])
                if p == 0:
                    pe.wait_ge(small_loaded, 48)

            def heads(p, i):
                for b in range(2):
                    n, u = W_PHASE[p] + b, p * P_HEADS + b
                    pe.wait_ge(w_loaded[b], i * 16 + 16 * (n // 2 + 1))
                    pe.wait_ge(s_read, i * 2 + (u + 1))
                    for j in range(2):
                        last = product(ps_q[:, b, j * P:(j + 1) * P], lambda k: wbuf[:, b, k, j * P:(j + 1) * P], lambda k: h_t[:, k, :])
                    last.then_inc(q_ps, 1)
                for b in range(2):
                    u = p * P_HEADS + b
                    pe.wait_ge(q_t_ready, i * 2 + (u + 1))
                    for j in range(2):
                        last = pe.matmul(ps_s[:, b, j * P:(j + 1) * P], q_t[:, b, j * P:(j + 1) * P], keys_sb[:, p // 2, j, :], start=True, stop=True)
                    last.then_inc(s_ps, 1)

            def open_sum(p):
                if p:
                    pe.wait_ge(x_ready, (0, 3, 5, 7)[p])
                pe.matmul(acc[:, :], ident[:, :], x_tok[:, p % 2, HALF:D], start=True, stop=False)

            def expert_round(p, i):
                for r in range(RING):
                    n = p * PICKS + r
                    pe.wait_ge(diag_ready, i * RING + (n + 1))
                    pe.matmul(acc[:, :], diag[:, r % (2 * BATCH), :], ring[:, r, D + HALF:2 * D], start=False, stop=False) \
                        .then_inc(v_multiplied, 1)

            def close_sum(p):
                pe.matmul(acc[:, :], zeros[:, :], x_tok[:, p % 2, HALF:D], start=False, stop=True).then_inc(acc_closed, 1)

            def conv_quad(t, i):
                for c in range(4):
                    n, m = W_CONV[t] + c, t * KD + c
                    pe.wait_ge(w_loaded[c % 2], i * 32 + 16 * (n // 2 + 1))
                    pe.wait_ge(glu_ready, i * 4 + (m + 1))
                    for j in range(2):
                        last = product(pm[:, c * 512 + j * P:c * 512 + (j + 1) * P],
                                       lambda k: wbuf[:, c % 2, k, j * P:(j + 1) * P], lambda k: h_t[:, k, :])
                    last.then_inc(pw_ps, 1)

            def conv_mean(t):
                pe.wait_ge(y_ready, 2 * (t + 1))
                product(pm[:, 0:P], lambda k: mean_w[:, :], lambda k: y_t[:, k, :]).then_inc(mu_ps, 1)

            def conv_variance(t):
                pe.wait_ge(ysq_ready, t + 1)
                product(pm[:, P:2 * P], lambda k: mean_w[:, :], lambda k: z_t[:, k, :]).then_inc(var_ps, 1)

            def conv_out(t):
                pe.wait_ge(z_ready, t + 1)
                for c in range(4):
                    n = 4 * t + c
                    w = chunk(W_CONV[t] + KD + c)
                    dst = pm[:, c * 512:c * 512 + WCOLS]
                    pe.matmul(dst, ones_row[:, :], b2_row[:, c * WCOLS:(c + 1) * WCOLS], start=True, stop=False)
                    for k in range(KD):
                        last = pe.matmul(dst, z_t[:, k, :], w[:, k, :], start=False, stop=(k == KD - 1))
                    last.then_inc(w2_ps, 1)

            norm_h_t(2)
            heads_start(0)
            open_sum(0)
            heads(0, 0)
            heads(0, 1)
            heads(0, 2)
            expert_round(0, 0)
            heads(0, 3)
            expert_round(0, 1)
            expert_round(0, 2)
            norm_h_t(3)
            heads_start(1)
            heads(1, 0)
            with pe.Fori(0, 3) as i:
                expert_round(0, i + 3)
                heads(1, i + 1)
            expert_round(0, 6)
            expert_round(0, 7)
            close_sum(0)
            for p in (1, 2):
                t = p - 1
                open_sum(p)
                norm_h_t(2 * p + 2)
                await_h_t(2 * p + 2)
                conv_quad(t, 0)
                expert_round(p, 0)
                conv_quad(t, 1)
                expert_round(p, 1)
                conv_mean(t)
                expert_round(p, 2)
                conv_variance(t)
                conv_out(t)
                expert_round(p, 3)
                norm_h_t(2 * p + 3)
                heads_start(p + 1)
                heads(p + 1, 0)
                with pe.Fori(0, 3) as i:
                    expert_round(p, i + 4)
                    heads(p + 1, i + 1)
                expert_round(p, 7)
                close_sum(p)
            open_sum(3)
            with pe.Fori(0, 8) as i:
                expert_round(3, i)
            close_sum(3)


def rotary_table():
    freq = (1.0 / (np.float32(10000.0) ** np.linspace(0.0, 1.0, R_D // 2, dtype=np.float32))).astype(np.float32)
    ang = (np.tile(freq, 2)[:, None] * np.arange(SEQ, dtype=np.float32)[None, :]).astype(np.float32)
    return np.stack([np.cos(ang), np.sin(ang)], axis=1).astype(np.float32)


def decay_table():
    log_g = np.log1p(-np.exp2(-5.0 - np.arange(R_HEADS)))
    diff = np.arange(P)[None, :] - np.arange(P)[:, None]
    near = np.where(diff[:, None, :] >= 0, np.exp(np.maximum(diff, 0)[:, None, :] * log_g[None, :, None]), 0.0)
    far = np.exp((diff + P)[:, None, :] * log_g[None, :, None])
    return (np.concatenate([near, near, far], axis=2) * R_D ** -0.5).astype(np.float32)


def kernel(**inputs):
    import concourse.bacc as bacc
    from concourse.bass_utils import run_bass_kernel_spmd

    a = {k: np.asarray(v) for k, v in inputs.items()}

    def channels(v):
        return v.reshape(-1, P).T

    taps = a["conv_dw"][0].T.reshape(KD, P, TAPS).transpose(1, 0, 2).reshape(P, KD * TAPS)
    arrays = {
        "x": a["x"][0],
        "gains": np.concatenate([a["mix_norm_e"], a["ffn_norm"][0:1], a["mix_norm_o"], a["ffn_norm"][1:2], a["final_norm"][None]]),
        "w_in": a["w_in"][0],
        "kv_norm": a["kv_norm"],
        "uk_t": a["w_uk"][0].transpose(0, 2, 1).reshape(4, P, LATENT).transpose(1, 0, 2),
        "uv_w": a["w_uv"][0].transpose(1, 0, 2).reshape(LATENT, A_HEADS * A_DIM),
        "w_o": a["w_o"][0],
        "rot": rotary_table(),
        "decay": decay_table(),
        "w1": a["conv_w1"][0].reshape(D, 2, KD, P).transpose(0, 2, 1, 3).reshape(D, 2 * D),
        "chan": np.concatenate([taps, channels(a["conv_b1"][0]), channels(a["conv_dw_b"][0]),
                                channels(a["conv_ln_g"][0]), channels(a["conv_ln_b"][0])], axis=1),
        "w2": a["conv_w2"][0],
        "b2": a["conv_b2"],
        "wq": a["peer_wq"],
        "keys_t": a["peer_keys"].transpose(3, 0, 1, 2),
        "experts0": np.concatenate([a["peer_u"][0], a["peer_v"][0]], axis=1),
        "experts1": np.concatenate([a["peer_u"][1], a["peer_v"][1]], axis=1),
    }
    arrays = {f"{n}_dram": np.ascontiguousarray(v) for n, v in arrays.items()}
    nc = bacc.Bacc("TRN2", target_bir_lowering=False, num_devices=1)
    args = [nc.dram_tensor(n, v.shape, mybir.dt.from_np(v.dtype), kind="ExternalInput").ap() for n, v in arrays.items()]
    out = nc.dram_tensor("out_dram", (SEQ, D), mybir.dt.float32, kind="ExternalOutput").ap()
    hybrid_decoder_trunk_kernel(nc, *args, out)
    r = run_bass_kernel_spmd(nc, [arrays], core_ids=[0])
    return r.results[0]["out_dram"].reshape(1, SEQ, D)
```

```python
import concourse.bass as bass
from concourse import mybir
from contextlib import ExitStack

import numpy as np

P = 128
D = 1024
KD = D // P
TILES = 2
SEQ = TILES * P
LAYERS = 2
A_HEADS, A_DIM, LATENT = 8, 64, 128
I_HEADS, I_DIM = 8, 32
TOPK = SEQ // 4
R_HEADS, R_D = 4, 128
TAPS = 31
HIST = TAPS - 1
P_HEADS, P_TOP = 8, 16
PICKS = P_HEADS * P_TOP
EPS = 1e-6
C_QA = 0
C_CKV = C_QA + A_HEADS * A_DIM
C_QI = C_CKV + LATENT
C_KI = C_QI + I_HEADS * I_DIM
C_WI = C_KI + I_DIM
C_RQ = C_WI + I_HEADS
C_RK = C_RQ + R_HEADS * R_D
C_RV = C_RK + R_HEADS * R_D
C_RG = C_RV + R_HEADS * R_D
C_END = C_RG + R_HEADS * R_D
W_PARTS = [(C_CKV, C_RQ), (C_QA, C_CKV), (C_RQ, C_RK), (C_RK, C_RV), (C_RV, C_RG), (C_RG, C_END)]

RING = 16
AHEAD = 5
BATCH = 4
HALF = D // 2
WCOLS = 256
WBUF = 2

MASKED = -(2.0 ** 126)
TAKEN = -(2.0 ** 127)
OFF = -1e30
LOWEST = -3e38

NORMS = [(0, 0), (0, 1), (1, 0), (1, 1), (2, 0), (3, 0), (2, 1), (3, 1), (4, 0), (4, 1)]
FIN = 8
GAIN_LOADS = [("norm", 0), ("norm", 2), ("norm", 4), ("bias", 0), ("norm", 5), ("norm", 6), ("bias", 1), ("norm", 7), ("norm", 8)]
SAME_GAIN = {1: 0, 3: 2, 9: 8}
X_OF_NORM = [0, 0, 1, 2, 3, 4, 5, 6, 7, 8]
W_O = [0, 8]
W_PHASE = [4, 16, 36, 56]
W_CONV = [24, 44]
CONV_INS = [(0, 0), (0, 1), (0, 3), (1, 0), (1, 1), (1, 2), (2, 0), (2, 1)]
CONV_GATES = [(0, 1), (0, 2), (1, 0), (1, 1), (1, 2), (1, 3), (2, 1), (2, 2)]
CP_DW, CP_BA, CP_BG, CP_DWB, CP_G, CP_B = 0, KD * TAPS, KD * TAPS + KD, KD * TAPS + 2 * KD, KD * TAPS + 3 * KD, KD * TAPS + 4 * KD
CP = CP_B + KD


def hybrid_decoder_trunk_kernel(nc, x, gains, w_in, kv_norm, uk_t, uv_w, w_o, rot, decay,
                                w1, chan, w2, b2, wq, keys_t, experts0, experts1, out):
    f32, u32 = mybir.dt.float32, mybir.dt.uint32
    ALU, ACT, AX = mybir.AluOpType, mybir.ActivationFunctionType, mybir.AxisListType
    ds = bass.ds

    w_in_v = w_in.rearrange("(k p) c -> p k c", p=P)
    w_o_v = w_o.rearrange("(k p) c -> p k c", p=P)
    w1_v = w1.rearrange("(k p) c -> p k c", p=P)
    w2_v = w2.rearrange("(k p) c -> p k c", p=P)
    wq_v = [wq[i, :, :].rearrange("(k p) c -> p k c", p=P) for i in range(LAYERS)]
    table = [experts0, experts1]

    ctx = ExitStack()
    with ctx:
        def sb(name, shape, dt=f32):
            return ctx.enter_context(nc.sbuf_tensor(name, shape, dt))

        def sem(name):
            return ctx.enter_context(nc.semaphore(name))

        ring = sb("ring", [P, RING, 2 * D])
        x_tok = sb("x_tok", [P, TILES, D])
        h_tok = sb("h_tok", [P, TILES, D])
        h_t = sb("h_t", [P, KD, P])
        gain = sb("gain", [P, 2, D])
        wbuf = sb("wbuf", [P, WBUF, KD, WCOLS])
        conv_buf = sb("conv_buf", [P, KD * (HIST + P) + KD * P])
        glu = conv_buf[:, 0:KD * (HIST + P)].rearrange("p (k c) -> p k c", k=KD)
        y_t = conv_buf[:, KD * (HIST + P):].rearrange("p (k c) -> p k c", k=KD)
        z_t = h_t
        chan_sb = sb("chan_sb", [P, CP])
        gate_sig = sb("gate_sig", [P, 4, P])
        rstd_y = sb("rstd_y", [P, P])
        mean_w = sb("mean_w", [P, P])
        ident = sb("ident", [P, P])
        iota16 = sb("iota16", [P, P_TOP])
        eps = sb("eps", [P, 1])
        keys_sb = sb("keys_sb", [P, LAYERS, 2, P])
        q_t = sb("q_t", [P, 2, 2 * P])
        top_v = sb("top_v", [P, 2, 2, P_TOP])
        top_i = sb("top_i", [P, 2, 2, P_TOP], u32)
        rest = sb("rest", [P, 2, 2, P])
        best_v = sb("best_v", [P, 2, P_TOP])
        best_i = sb("best_i", [P, 2, P_TOP], u32)
        best_ab = sb("best_ab", [P, 2, 2, P_TOP], u32)
        onehot = sb("onehot", [P, 2, 2, P_TOP, P_TOP])
        e12 = sb("e12", [P, 2, 2, P_TOP])
        lead = sb("lead", [P, 2, P_TOP])
        expo = sb("expo", [P, 2, P_TOP])
        expo_sum = sb("expo_sum", [P, 2])
        gates = sb("gates", [P, TILES, PICKS])
        eidx = sb("eidx", [P, TILES, PICKS], u32)
        idx_now = sb("idx_now", [P, 2, RING], u32)
        hb = sb("hb", [P, RING])
        ge = sb("ge", [P, RING])
        act_v = sb("act_v", [P, RING])
        diag = sb("diag", [P, 2 * BATCH, P])
        ss = sb("ss", [P, len(NORMS)])
        root = sb("root", [P, len(NORMS)])
        rstd = sb("rstd", [P, len(NORMS)])

        ring_flat = ring[:, :, :].rearrange("p r c -> p (r c)")
        at = [0]

        def in_ring(*dims):
            n = int(np.prod(dims))
            v = ring_flat[:, at[0]:at[0] + n]
            at[0] += n
            names = "abcd"[:len(dims)]
            sizes = {names[i]: dims[i] for i in range(len(dims) - 1)}
            return v if len(dims) == 1 else v.rearrange(f"p ({' '.join(names)}) -> p {' '.join(names)}", **sizes)

        w_part = [in_ring(KD, b - a) for a, b in W_PARTS]
        w_end = at[0]
        at[0] = 0
        rel = [in_ring(I_HEADS * P * (t + 1)) for t in range(TILES)]
        at[0] = 0
        logit, p_t, o_t = [in_ring(A_HEADS * P)], [in_ring(1, A_HEADS * P)], [in_ring(A_HEADS * P)]
        at[0] = 0
        p_t.append(in_ring(2, A_HEADS * P))
        o_t.append(in_ring(A_HEADS * P))
        assert at[0] <= KD * (C_RQ - C_CKV)
        decay_sb = [wbuf[:, 0, :, :].rearrange("p k c -> p (k c)")[:, 0:R_HEADS * P].rearrange("p (h c) -> p h c", h=R_HEADS)]
        at[0] = KD * (C_RQ - C_CKV)
        ql_t = [h_tok[:, 0, :], in_ring(A_HEADS * P)]
        logit.append(in_ring(A_HEADS * SEQ))
        assert at[0] <= KD * (C_RQ - C_CKV + C_CKV)
        part = KD * R_HEADS * R_D
        in_use = {(w_end - n * part) // (2 * D): job for n, job in ((4, ("rq", 1)), (2, ("rv", 1)), (1, ("rg", 1)), (0, None))}
        at[0] = w_end
        qa_t = in_ring(4, SEQ)
        qi_t = in_ring(2, SEQ)
        s_t = [h_tok[:, 1, 0:R_HEADS * P].rearrange("p (h c) -> p h c", h=R_HEADS), qa_t]
        b_tok = [h_tok[:, 1, R_HEADS * P:2 * R_HEADS * P], qi_t.rearrange("p a c -> p (a c)")]
        ki_t = in_ring(SEQ)
        rqk = in_ring(2, 2, 2, SEQ)
        rv = in_ring(TILES, R_HEADS * R_D)
        rg = in_ring(TILES, R_HEADS * R_D)
        uvw_sb = in_ring(A_HEADS * A_DIM)
        c_tok = in_ring(TILES, LATENT)
        c_t = in_ring(SEQ)
        wi = in_ring(TILES, I_HEADS)
        rot_sb = in_ring(2, SEQ)
        dead_at = at[0]
        ukt_sb = in_ring(4, LATENT)
        score = in_ring(TILES, SEQ)
        decay_sb.append(ring_flat[:, dead_at:dead_at + R_HEADS * 2 * P].rearrange("p (h c) -> p h c", h=R_HEADS))
        assert at[0] <= RING * 2 * D, at[0]
        h_in = [conv_buf[:, t * D:(t + 1) * D].rearrange("p (k c) -> p k c", k=KD) for t in range(TILES)]
        mix_t = [h_in[0], h_in[0]]
        ki_w = h_t
        in_diag = diag[:, :, :].rearrange("p k c -> p (k c)")
        rot_cos = onehot[:, 0, :, :, :].rearrange("p a b c -> p (a b c)").rearrange("p (a i c) -> p a i c", a=2, i=2)
        rot_sin = in_diag[:, 0:2 * SEQ].rearrange("p (a i c) -> p a i c", a=2, i=2)
        kvg = in_diag[:, 2 * SEQ:2 * SEQ + LATENT]
        ckv_raw = in_diag[:, 3 * SEQ:3 * SEQ + TILES * LATENT].rearrange("p (t c) -> p t c", t=TILES)
        mask = gate_sig[:, :, :].rearrange("p k c -> p (k c)").rearrange("p (t c) -> p t c", t=TILES)
        best8 = rstd_y[:, 0:8]
        row_max = rstd_y[:, 8:16]
        row_sum = rstd_y[:, 16:24]
        row_inv = rstd_y[:, 24:32]
        gn_stat = rstd_y[:, 32:80].rearrange("p (g s) -> p g s", s=6)
        gn_mv = rstd_y[:, 80:96].rearrange("p (g s) -> p g s", s=2)
        gn_root = rstd_y[:, 96:104]
        gn_rstd = rstd_y[:, 104:112]
        c_ss = rstd_y[:, 112:114]
        c_root = rstd_y[:, 114:116]
        c_rstd = rstd_y[:, 116:118]

        side = ctx.enter_context(nc.psum_tensor("side", [P, 4, 512], f32))
        side_flat = side[:, :, :].rearrange("p b c -> p (b c)")
        ps_s = side[:, 0:2, :]
        ps_q = side[:, 0:2, 2 * P:4 * P]
        acc = side[:, 2, :]
        cand = side[:, 3, :].rearrange("p (h a b) -> p h a b", h=2, a=P_TOP)
        pm = ctx.enter_context(nc.psum_tensor("pm", [P, 4 * 512], f32))

        x_loaded = [sem(f"x_loaded{t}") for t in range(TILES)]
        w_in_loaded = [sem(f"w_in_loaded{i}") for i in range(len(W_PARTS))]
        rot_loaded, uk_loaded, small_loaded, decay_loaded = sem("rot_loaded"), sem("uk_loaded"), sem("small_loaded"), sem("decay_loaded")
        const_ready = sem("const_ready")
        gain_loaded = [sem(f"gain_loaded{i}") for i in range(2)]
        norm_root, h_ready, h_t_ps, h_t_ready = sem("norm_root"), sem("h_ready"), sem("h_t_ps"), sem("h_t_ready")
        x_ready = sem("x_ready")
        bias_added = sem("bias_added")
        proj_ps = sem("proj_ps")
        proj_read = [sem(f"proj_read{b}") for b in range(4)]
        ckv_root, c_ready = sem("ckv_root"), sem("c_ready")
        idx_ps, rel_ready, score_ready, causal_ready = sem("idx_ps"), sem("rel_ready"), sem("score_ready"), sem("causal_ready")
        taken_ready, mask_ready = sem("taken_ready"), sem("mask_ready")
        rot_ready = sem("rot_ready")
        ki_copied = sem("ki_copied")
        rg_sig = sem("rg_sig")
        ret_s_ps, ret_s_ready, ret_ps = sem("ret_s_ps"), sem("ret_s_ready"), sem("ret_ps")
        gn_var, gn_rooted, b_ready, b_t_ps, b_t_ready = sem("gn_var"), sem("gn_rooted"), sem("b_ready"), sem("b_t_ps"), sem("b_t_ready")
        ql_ps, ql_ready = sem("ql_ps"), sem("ql_ready")
        logit_ps, logit_ready, expo_ready, prob_ready = sem("logit_ps"), sem("logit_ready"), sem("expo_ready"), sem("prob_ready")
        p_t_ps, p_t_ready, o_ps, o_ready, a_ps, a_ready = (sem(n) for n in ("p_t_ps", "p_t_ready", "o_ps", "o_ready", "a_ps", "a_ready"))
        wo_ps = sem("wo_ps")
        w_loaded = [sem(f"w_loaded{i}") for i in range(WBUF)]
        q_ps, q_t_ready, s_ps, s_read, topk_on = sem("q_ps"), sem("q_t_ready"), sem("s_ps"), sem("s_read"), sem("topk_on")
        lead_ready, gate_exp, picks_ready = sem("lead_ready"), sem("gate_exp"), sem("picks_ready")
        gathered = [sem(f"gathered{r}") for r in range(RING)]
        idx_copied, may_gather = sem("idx_copied"), sem("may_gather")
        dots_ready, act_ready, diag_ready, v_added, v_multiplied = (sem(n) for n in ("dots_ready", "act_ready", "diag_ready", "v_added", "v_multiplied"))
        pw_ps, sig_ready, glu_ready = sem("pw_ps"), sem("sig_ready"), sem("glu_ready")
        conv_steps, mu_ps, yc_ready, ysq_ready, var_ps, root_ready, u_ready, zsig_ready, z_ready = (
            sem(n) for n in ("conv_steps", "mu_ps", "yc_ready", "ysq_ready", "var_ps", "root_ready", "u_ready", "zsig_ready", "z_ready"))
        w2_ps = sem("w2_ps")
        stored = sem("stored")

        block = ctx.enter_context(nc.Block())

        retention_ps = [side[:, 0:2, :], pm[:, 512:1536].rearrange("p (b c) -> p b c", b=2)]
        retained_ps = [side_flat[:, 1024:1536], pm[:, 1536:2048]]
        b_t_at = [side_flat[:, 0:512], pm[:, 0:512]]
        absorbed_ps = [side[:, 0:2, :], pm[:, 1024:2048].rearrange("p (b c) -> p b c", b=2)]
        logits_at = [side_flat[:, 0:A_HEADS * P], pm[:, 0:A_HEADS * SEQ]]
        p_t_at = [side_flat[:, 1024:2048], pm[:, :]]
        o_at = [side_flat[:, 0:1024], pm[:, 512:1536]]
        a_at = [side_flat[:, 1536:2048], pm[:, 1536:2048]]
        wo_at = [[side_flat[:, c * 512:c * 512 + WCOLS] for c in range(4)], [pm[:, c * 512:c * 512 + WCOLS] for c in range(4)]]

        def norm_at(e):
            return side_flat[:, 1024:2048] if e == 2 else pm[:, 1024:2048] if e == 1 else pm[:, 0:1024]

        def head_slot(h):
            return (h % 2) * 2 + h // 2

        PROJ = [("ckv", 0, 0), ("ckv", 1, 0), ("qi", 0, 0), ("ki", 0, 0), ("qi", 1, 0), ("ki", 1, 0), ("qa", 0, 1), ("c_t", 0, 0),
                ("rq", 0, 2), ("rk", 0, 3), ("rv", 0, 4), ("rg", 0, 5),
                ("qa", 1, 1), ("rk", 1, 3), ("rq", 1, 2), ("rv", 1, 4), ("rg", 1, 5)]

        def job_of(kind, i=0):
            return next(n for n, (k, j, _) in enumerate(PROJ) if (k, j) == (kind, i))

        @block.sync
        def _(sp):
            for t in range(TILES):
                sp.dma_start(x_tok[:, t, :], x[t * P:(t + 1) * P, :]).then_inc(x_loaded[t], 16)
                if t == 0:
                    sp.dma_start(gain[:, 0, :], gains[0:1, :].broadcast_to([P, D])).then_inc(gain_loaded[0], 16)
            for i, (a, b) in enumerate(W_PARTS):
                sp.dma_start(w_part[i], w_in_v[:, :, a:b]).then_inc(w_in_loaded[i], 16)
                if i == 0:
                    sp.dma_start(kvg, kv_norm.broadcast_to([P, LATENT])).then_inc(uk_loaded, 16)
                    sp.dma_start(ukt_sb, uk_t).then_inc(uk_loaded, 16)
                    sp.dma_start(uvw_sb, uv_w).then_inc(uk_loaded, 16)
                    sp.dma_start(rot_sb, rot).then_inc(rot_loaded, 16)
                    sp.dma_start(decay_sb[0], decay[:, :, 0:P]).then_inc(decay_loaded, 16)
            sp.dma_start(keys_sb[:, :, :, :], keys_t).then_inc(small_loaded, 16)
            sp.dma_start(chan_sb[:, :], chan).then_inc(small_loaded, 16)

            def load_gain(kind, e):
                g = GAIN_LOADS.index((kind, e))
                if g >= 2:
                    user, of = GAIN_LOADS[g - 2]
                    of = max([of] + [n for n, first in SAME_GAIN.items() if user == "norm" and first == of])
                    sp.wait_ge(h_ready if user == "norm" else bias_added, of + 1)
                row = gains[NORMS[e][0]:NORMS[e][0] + 1, :] if kind == "norm" else b2
                sp.dma_start(gain[:, g % 2, :], row.broadcast_to([P, D])).then_inc(gain_loaded[g % 2], 16)

            def multiplied(n):
                if n < W_PHASE[0]:
                    return wo_ps, n + 1
                if n < W_PHASE[1]:
                    kinds = (["q"] * 2 + ["q", "q", "o", "o"] * 2 + ["q"] * 2)[:n - W_PHASE[0] + 1]
                    return (q_ps, kinds.count("q")) if kinds[-1] == "q" else (wo_ps, 4 + kinds.count("o"))
                for p, first in enumerate(W_PHASE):
                    if first <= n < first + P_HEADS:
                        return q_ps, p * P_HEADS + n - first + 1
                for t, first in enumerate(W_CONV):
                    if first <= n < first + KD:
                        return pw_ps, t * KD + n - first + 1
                    if first + KD <= n < first + KD + 4:
                        return w2_ps, t * 4 + n - first - KD + 1

            def load_chunks(view, first, end, start=0):
                for c in range(start, end):
                    n = first + c
                    if n >= WBUF:
                        sp.wait_ge(*multiplied(n - WBUF))
                    else:
                        sp.wait_ge(ret_s_ready, 1)
                    sp.dma_start(wbuf[:, n % WBUF, :, :], view[:, :, c * WCOLS:(c + 1) * WCOLS]) \
                      .then_inc(w_loaded[n % WBUF], 16)

            load_gain("norm", 2)
            load_chunks(w_o_v, W_O[0], 2)
            sp.wait_ge(ql_ps, 2)
            sp.wait_ge(taken_ready, 2)
            sp.dma_start(decay_sb[1], decay).then_inc(decay_loaded, 16)
            load_chunks(w_o_v, W_O[0], 4, 2)
            load_chunks(wq_v[0], W_PHASE[0], 4)
            load_chunks(w_o_v, W_O[1], 2)
            load_chunks(wq_v[0], W_PHASE[0] + 2, 6, 4)
            load_chunks(w_o_v, W_O[1] + 2, 4, 2)
            load_chunks(wq_v[0], W_PHASE[0] + 4, 8, 6)
            load_gain("norm", 4)
            load_chunks(wq_v[0], W_PHASE[1], P_HEADS)
            load_gain("bias", 0)
            load_chunks(w1_v, W_CONV[0], KD)
            load_gain("norm", 5)
            load_chunks(w2_v, W_CONV[0] + KD, 4)
            load_chunks(wq_v[1], W_PHASE[2], 2)
            load_gain("norm", 6)
            load_chunks(wq_v[1], W_PHASE[2], P_HEADS, 2)
            load_gain("bias", 1)
            load_chunks(w1_v, W_CONV[1], KD)
            load_gain("norm", 7)
            load_chunks(w2_v, W_CONV[1] + KD, 4)
            load_chunks(wq_v[1], W_PHASE[3], 2)
            load_gain("norm", 8)
            load_chunks(wq_v[1], W_PHASE[3], P_HEADS, 2)
            for t in range(TILES):
                sp.wait_ge(h_ready, FIN + t + 1)
                sp.dma_start(out[t * P:(t + 1) * P, :], h_tok[:, t, :]).then_inc(stored, 16)
            sp.wait_ge(stored, 16 * TILES)

        @block.gpsimd
        def _(pool):
            pool.memset(ident[:, :], 1.0)
            pool.memset(mean_w[:, :], 1.0 / D)
            pool.memset(eps[:, :], EPS)
            pool.iota(iota16[:, :], [[1, P_TOP]], base=0, channel_multiplier=0,
                      allow_small_or_imprecise_dtypes=True).then_inc(const_ready, 1)
            pool.wait_ge(const_ready, 1)
            pool.affine_select(out=ident[:, :], in_=ident[:, :], compare_op=ALU.is_equal, fill=0.0, base=0,
                               pattern=[[-1, P]], channel_multiplier=1).then_inc(const_ready, 1)
            c0 = C_KI - C_CKV
            pool.wait_ge(w_in_loaded[0], 16)
            for k in range(KD):
                last = pool.tensor_copy(ki_w[:, k, :].rearrange("p (g c) -> p g c", g=4),
                                        w_part[0][:, k, c0:c0 + I_DIM].unsqueeze(1).broadcast_to([P, 4, I_DIM]))
            last.then_inc(ki_copied, 1)
            for t in range(TILES):
                s = P * (t + 1)
                for src, ready, fill, done in ((score, score_ready, MASKED, causal_ready), (mask, taken_ready, OFF, mask_ready)):
                    pool.wait_ge(ready, t + 1)
                    pool.affine_select(out=src[:, t, 0:s], in_=src[:, t, 0:s], compare_op=ALU.is_ge, fill=fill,
                                       base=P * t, pattern=[[-1, s]], channel_multiplier=1).then_inc(done, 1)

            def gathers(p):
                layer, t = p // 2, p % 2
                rounds = PICKS // RING
                with pool.Fori(0, rounds // 2) as i:
                    for half in range(2):
                        r0 = p * rounds + half
                        pool.wait_ge(picks_ready, i * 2 + (r0 + 1))
                        pool.wait_ge(v_added, i * (2 * RING) + (r0 * RING + 1))
                        pool.sem_inc(may_gather, 1)
                        pool.tensor_copy(idx_now[:, half, :], eidx[:, t, ds(i * (2 * RING) + half * RING, RING)]) \
                            .then_inc(idx_copied, 1)
                        pool.wait_ge(idx_copied, i * 2 + (r0 + 1))
                        for r in range(RING):
                            freed = r0 * RING + r + 1
                            pool.wait_ge(v_added, i * (2 * RING) + freed)
                            pool.wait_ge(v_multiplied, i * (2 * RING) + freed)
                            if p == 0 and half == 0 and r in in_use:
                                if in_use[r]:
                                    pool.wait_ge(proj_ps, job_of(*in_use[r]) + 1)
                                else:
                                    pool.wait_ge(b_t_ready, 2)
                            if r >= AHEAD:
                                pool.wait_ge(gathered[r - AHEAD], i * 32 + 16 * (r0 + 1))
                            elif p or half:
                                pool.wait_ge(gathered[r - AHEAD + RING], i * 32 + 16 * r0)
                            pool.sem_inc(may_gather, 1)
                            pool.indirect_dma_start(ring[:, r, :], None, table[layer],
                                                    bass.IndirectOffsetOnAxis(idx_now[:, half, r:r + 1], 0)) \
                                .then_inc(gathered[r], 16)

            pool.wait_ge(a_ready, 2)
            for p in range(2 * LAYERS):
                gathers(p)

        @block.scalar
        def _(act):
            def norm(e):
                t = NORMS[e][1]
                if e < 2:
                    act.wait_ge(x_loaded[t], 16)
                else:
                    act.wait_ge(x_ready, X_OF_NORM[e])
                act.activation(h_tok[:, t, :], x_tok[:, t, :], ACT.Square, accum_out=ss[:, e:e + 1])
                act.drain()
                act.activation(root[:, e:e + 1], ss[:, e:e + 1], ACT.Sqrt, bias=eps[:, :], scale=1.0 / D).then_inc(norm_root, 1)

            def keep_h_t(e, dst):
                act.wait_ge(h_t_ps, e + 1)
                act.copy(dst, norm_at(e).rearrange("p (k c) -> p k c", k=KD)).then_inc(h_t_ready, 1)

            act.wait_ge(const_ready, 2)
            norm(0)
            norm(1)
            keep_h_t(0, h_in[0])
            keep_h_t(1, h_in[1])

            def read(kind, t):
                n = job_of(kind, t)
                act.wait_ge(proj_ps, n + 1)
                return pm[:, (n % 4) * 512:(n % 4) * 512 + 512], proj_read[n % 4]

            def columns(t):
                return slice(t * P, (t + 1) * P)

            def keep_latents(t):
                ps, done = read("ckv", t)
                act.copy(ckv_raw[:, t, :], ps[:, 0:LATENT])
                act.mul(wi[:, t, :].rearrange("p (a b) -> p a b", a=4),
                        ps[:, LATENT:LATENT + I_HEADS].rearrange("p (b a) -> p a b", a=4), I_HEADS ** -0.5).then_inc(done, 1)
                act.drain()
                act.activation(c_tok[:, t, :], ckv_raw[:, t, :], ACT.Square, accum_out=c_ss[:, t:t + 1])
                act.drain()
                act.activation(c_root[:, t:t + 1], c_ss[:, t:t + 1], ACT.Sqrt, bias=eps[:, :], scale=1.0 / LATENT).then_inc(ckv_root, 1)

            def keep_index(t):
                ps, done = read("qi", t)
                act.copy(qi_t[:, :, columns(t)], ps[:, 0:2 * P].rearrange("p (k c) -> p k c", k=2)).then_inc(done, 1)
                ps, done = read("ki", t)
                act.copy(ki_t[:, columns(t)], ps[:, 0:P]).then_inc(done, 1)

            def relu_index(t):
                s = P * (t + 1)
                act.wait_ge(idx_ps, t + 1)
                act.activation(rel[t].rearrange("p (a c) -> p a c", a=4), side[:, :, 0:2 * s], ACT.Relu).then_inc(rel_ready, 1)

            def keep_qa(t):
                ps, done = read("qa", t)
                act.copy(qa_t[:, :, columns(t)], ps[:, :].rearrange("p (k c) -> p k c", k=4)).then_inc(done, 1)

            def keep_rv(t):
                ps, done = read("rv", t)
                act.copy(rv[:, t, :], ps[:, :]).then_inc(done, 1)

            def gate_of_retention(t):
                n = job_of("rg", t)
                act.wait_ge(proj_ps, n + 1)
                act.activation(rg[:, t, :], pm[:, (n % 4) * 512:(n % 4) * 512 + 512], ACT.Sigmoid).then_inc(rg_sig, 1)

            def root_of_group_norm(t):
                g = slice(t * R_HEADS, (t + 1) * R_HEADS)
                act.wait_ge(gn_var, t + 1)
                act.activation(gn_root[:, g], gn_mv[:, g, 1:2].rearrange("p g s -> p (g s)"), ACT.Sqrt, bias=eps[:, :]).then_inc(gn_rooted, 1)

            def keep_retained(t):
                act.wait_ge(b_t_ps, t + 1)
                act.copy(mix_t[t][:, 4:8, :], b_t_at[t].rearrange("p (k c) -> p k c", k=4)).then_inc(b_t_ready, 1)

            def keep_absorbed(t):
                act.wait_ge(ql_ps, t + 1)
                act.copy(ql_t[t].rearrange("p (b c) -> p b c", b=2), absorbed_ps[t]).then_inc(ql_ready, 1)

            def exp_logits(t):
                act.wait_ge(logit_ready, t + 1)
                act.activation(logit[t], logit[t], ACT.Exp).then_inc(expo_ready, 1)

            def keep_probs(t):
                act.wait_ge(p_t_ps, t + 1)
                act.copy(p_t[t], p_t_at[t].rearrange("p (s c) -> p s c", s=t + 1)).then_inc(p_t_ready, 1)

            def keep_latent_sums(t):
                act.wait_ge(o_ps, t + 1)
                act.copy(o_t[t], o_at[t]).then_inc(o_ready, 1)

            def keep_attended(t):
                act.wait_ge(a_ps, t + 1)
                act.copy(mix_t[t][:, 0:4, :], a_at[t].rearrange("p (k c) -> p k c", k=4)).then_inc(a_ready, 1)

            keep_latents(0)
            keep_latents(1)
            keep_index(0)
            keep_index(1)
            relu_index(0)
            keep_qa(0)
            ps, done = read("c_t", 0)
            act.copy(c_t, ps[:, 0:SEQ]).then_inc(done, 1)
            relu_index(1)
            keep_absorbed(0)
            exp_logits(0)
            keep_rv(0)
            gate_of_retention(0)
            keep_probs(0)
            keep_latent_sums(0)
            root_of_group_norm(0)
            keep_qa(1)
            keep_attended(0)
            keep_retained(0)
            keep_absorbed(1)

            def keep_input(e):
                keep_h_t(e, h_t[:, :, :])

            def keep_query(p, i, b):
                u = p * P_HEADS + b
                act.wait_ge(q_ps, i * 2 + (u + 1))
                act.copy(q_t[:, b, :], ps_q[:, b, :]).then_inc(q_t_ready, 1)

            def gate_exps(p, i, pair=(0, 1)):
                for b in pair:
                    act.wait_ge(lead_ready, i * 2 + (p * P_HEADS + b + 1))
                    act.activation(expo[:, b, :], lead[:, b, :], ACT.Exp, accum_out=expo_sum[:, b:b + 1]).then_inc(gate_exp, 1)

            def expert_round(p, i, between=None):
                t = p % 2
                for b in range(RING // BATCH):
                    n0 = p * PICKS + b * BATCH
                    c = slice(b * BATCH, (b + 1) * BATCH)
                    act.wait_ge(dots_ready, i * RING + (n0 + BATCH))
                    act.activation(ge[:, c], hb[:, c], ACT.Gelu)
                    act.drain()
                    for j in range(BATCH):
                        r = b * BATCH + j
                        last = act.activation(act_v[:, r:r + 1], ge[:, r:r + 1], ACT.Copy,
                                              scale=gates[:, t, ds(i * RING + r, 1)])
                    last.then_inc(act_ready, BATCH)
                    act.drain()
                    act.wait_ge(v_multiplied, i * RING + (RING + n0 - BATCH))
                    for j in range(BATCH):
                        r = b * BATCH + j
                        act.activation(diag[:, (b % 2) * BATCH + j, :], ident[:, :], ACT.Copy,
                                       scale=act_v[:, r:r + 1]).then_inc(diag_ready, 1)
                    if between:
                        between(b)
                act.drain()

            def gate_of_glu(t, n):
                c = n % 4
                act.wait_ge(pw_ps, t * KD + n + 1)
                act.wait_ge(glu_ready, t * KD + n + 1)
                act.activation(gate_sig[:, c, :], pm[:, c * 512 + P:c * 512 + 2 * P], ACT.Sigmoid,
                               bias=chan_sb[:, CP_BG + n:CP_BG + n + 1]).then_inc(sig_ready, 1)

            def conv_square(t):
                act.wait_ge(yc_ready, t + 1)
                act.activation(z_t[:, :, :], y_t[:, :, :], ACT.Square).then_inc(ysq_ready, 1)

            def conv_root(t):
                act.wait_ge(var_ps, t + 1)
                act.activation(rstd_y[:, :], pm[:, P:2 * P], ACT.Sqrt, bias=eps[:, :]).then_inc(root_ready, 1)

            def conv_swish(t):
                act.wait_ge(u_ready, t + 1)
                act.activation(z_t[:, :, :], y_t[:, :, :], ACT.Sigmoid).then_inc(zsig_ready, 1)

            def conv_beside(t, i, b):
                if (i, b) in CONV_GATES:
                    gate_of_glu(t, CONV_GATES.index((i, b)))
                elif (i, b) == (3, 0):
                    conv_root(t)
                elif (i, b) == (3, 1):
                    conv_swish(t)

            norm(2)
            exp_logits(1)
            keep_input(2)
            keep_query(0, 0, 0)
            keep_probs(1)
            gate_exps(0, 0, (0,))
            keep_latent_sums(1)
            keep_query(0, 0, 1)
            keep_attended(1)
            gate_exps(0, 0, (1,))
            keep_rv(1)
            root_of_group_norm(1)
            gate_of_retention(1)
            keep_retained(1)
            expert_round(0, 0, lambda b: keep_query(0, 1, b - 1) if b in (1, 2) else None)
            gate_exps(0, 1)
            expert_round(0, 1, lambda b: keep_query(0, 2, b - 1) if b in (1, 2) else None)
            gate_exps(0, 2)
            norm(3)
            expert_round(0, 2, lambda b: keep_query(0, 3, b - 1) if b in (1, 2) else None)
            gate_exps(0, 3)
            keep_input(3)
            with act.Fori(0, 4) as i:
                expert_round(0, i + 3, lambda b: keep_query(1, i, b - 1) if b in (1, 2) else None)
                gate_exps(1, i)
            expert_round(0, 7)
            for p in (1, 2):
                t = p - 1
                norm(2 * p + 2)
                keep_input(2 * p + 2)
                for i in range(4):
                    expert_round(p, i, lambda b: conv_beside(t, i, b))
                    if i == 2:
                        conv_square(t)
                norm(2 * p + 3)
                keep_input(2 * p + 3)
                with act.Fori(0, 4) as i:
                    expert_round(p, i + 4, lambda b: keep_query(p + 1, i, b - 1) if b in (1, 2) else None)
                    gate_exps(p + 1, i)
            norm(8)
            with act.Fori(0, 8) as i:
                expert_round(3, i)
            act.activation(root[:, 9:10], eps[:, :], ACT.Sqrt)
            act.drain()
            norm(9)

        @block.vector
        def _(dve):
            def norm(e):
                t = NORMS[e][1]
                dve.wait_ge(norm_root, e + 1)
                dve.reciprocal(rstd[:, e:e + 1], root[:, e:e + 1])
                dve.drain()
                g = GAIN_LOADS.index(("norm", SAME_GAIN.get(e, e)))
                dve.wait_ge(gain_loaded[g % 2], 16 * (g // 2 + 1))
                dve.scalar_tensor_tensor(out=h_tok[:, t, :], in0=x_tok[:, t, :], scalar=rstd[:, e:e + 1],
                                         in1=gain[:, g % 2, :], op0=ALU.mult, op1=ALU.mult).then_inc(h_ready, 1)

            dve.sem_inc(s_read, 2)
            dve.sem_inc(glu_ready, 4)
            dve.sem_inc(v_added, RING)
            norm(0)
            norm(1)
            dve.wait_ge(uk_loaded, 48)
            for t in range(TILES):
                dve.wait_ge(ckv_root, t + 1)
                dve.reciprocal(c_rstd[:, t:t + 1], c_root[:, t:t + 1])
                dve.drain()
                dve.scalar_tensor_tensor(out=c_tok[:, t, :], in0=ckv_raw[:, t, :], scalar=c_rstd[:, t:t + 1],
                                         in1=kvg, op0=ALU.mult, op1=ALU.mult).then_inc(c_ready, 1)

            def rotary(t, j):
                n = job_of(("rq", "rk")[j], t)
                dve.wait_ge(proj_ps, n + 1)
                dve.wait_ge(rot_loaded, 16)
                ps = pm[:, (n % 4) * 512:(n % 4) * 512 + 512].rearrange("p (i a c) -> p i a c", i=2, a=2)
                tok = slice(t * P, (t + 1) * P)
                cos, sin = (rot_sb[:, w, tok].unsqueeze(1).broadcast_to([P, 2, P]) for w in range(2))
                for a in range(2):
                    dve.tensor_tensor(rot_cos[:, a, :, :], ps[:, :, a, :], cos, ALU.mult)
                    last = dve.tensor_tensor(rot_sin[:, a, :, :], ps[:, :, 1 - a, :], sin, ALU.mult)
                last.then_inc(proj_read[n % 4], 1)
                dve.drain()
                dve.tensor_tensor(rqk[:, j, :, 0, tok], rot_cos[:, 0, :, :], rot_sin[:, 0, :, :], ALU.subtract)
                dve.tensor_tensor(rqk[:, j, :, 1, tok], rot_cos[:, 1, :, :], rot_sin[:, 1, :, :], ALU.add).then_inc(rot_ready, 1)
                dve.drain()

            def swish_of_retention(t):
                n = job_of("rg", t)
                dve.wait_ge(rg_sig, t + 1)
                dve.tensor_tensor(rg[:, t, :], pm[:, (n % 4) * 512:(n % 4) * 512 + 512], rg[:, t, :], ALU.mult) \
                    .then_inc(proj_read[n % 4], 1)

            def index_scores(t):
                s = P * (t + 1)
                dve.wait_ge(rel_ready, t + 1)
                heads_rel = rel[t].rearrange("p (h s) -> p h s", h=I_HEADS)
                dve.tensor_tensor(heads_rel, heads_rel, wi[:, t, :].unsqueeze(2).broadcast_to([P, I_HEADS, s]), ALU.mult)
                dve.drain()
                dve.tensor_reduce(score[:, t, 0:s], rel[t].rearrange("p (h s) -> p s h", h=I_HEADS), AX.X, ALU.add) \
                   .then_inc(score_ready, 1)

            def take_top(t):
                s = P * (t + 1)
                dve.wait_ge(causal_ready, t + 1)
                for _ in range(TOPK // 8):
                    dve.max(best8, score[:, t, 0:s])
                    dve.drain()
                    dve.match_replace(score[:, t, 0:s], best8, score[:, t, 0:s], TAKEN)
                    dve.drain()
                dve.tensor_scalar(mask[:, t, 0:s], score[:, t, 0:s], TAKEN, OFF, ALU.not_equal, ALU.mult).then_inc(taken_ready, 1)

            def decay_scores(t):
                dve.wait_ge(ret_s_ps, t + 1)
                dve.wait_ge(decay_loaded, 16 * (t + 1))
                w = P * (t + 1)
                dve.tensor_tensor(s_t[t].rearrange("p (b h) c -> p b h c", b=2),
                                  retention_ps[t][:, :, 0:2 * w].rearrange("p b (h c) -> p b h c", h=2),
                                  decay_sb[t].rearrange("p (b h) c -> p b h c", b=2), ALU.mult).then_inc(ret_s_ready, 1)

            def group_norm(t):
                ps = retained_ps[t]
                of_tile = slice(t * R_HEADS, (t + 1) * R_HEADS)
                dve.wait_ge(ret_ps, t + 1)
                for h in range(R_HEADS):
                    dve.bn_stats(gn_stat[:, t * R_HEADS + h, :], ps[:, h * R_D:(h + 1) * R_D])
                dve.drain()
                for h in range(R_HEADS):
                    last = dve.bn_aggr(gn_mv[:, t * R_HEADS + h, :], gn_stat[:, t * R_HEADS + h, :])
                last.then_inc(gn_var, 1)
                dve.wait_ge(gn_rooted, t + 1)
                dve.reciprocal(gn_rstd[:, of_tile], gn_root[:, of_tile])
                dve.drain()
                for h in range(R_HEADS):
                    g = t * R_HEADS + h
                    dve.tensor_scalar(b_tok[t][:, h * R_D:(h + 1) * R_D], ps[:, h * R_D:(h + 1) * R_D],
                                      gn_mv[:, g, 0:1], gn_rstd[:, g:g + 1], ALU.subtract, ALU.mult)

            def gate_retained(t):
                dve.drain()
                dve.tensor_tensor(b_tok[t], b_tok[t], rg[:, t, :], ALU.mult).then_inc(b_ready, 1)

            def logits(t):
                s = P * (t + 1)
                lg = logit[t].rearrange("p (h s) -> p h s", h=A_HEADS)
                dve.wait_ge(logit_ps, t + 1)
                dve.wait_ge(mask_ready, t + 1)
                dve.scalar_tensor_tensor(out=lg, in0=logits_at[t].rearrange("p (h s) -> p h s", h=A_HEADS),
                                         scalar=A_DIM ** -0.5, in1=mask[:, t, 0:s].unsqueeze(1).broadcast_to([P, A_HEADS, s]),
                                         op0=ALU.mult, op1=ALU.add)
                dve.drain()
                dve.tensor_reduce(row_max, lg, AX.X, ALU.max)
                dve.drain()
                dve.tensor_tensor(lg, lg, row_max.unsqueeze(2).broadcast_to([P, A_HEADS, s]), ALU.subtract).then_inc(logit_ready, 1)

            def probs(t):
                s = P * (t + 1)
                lg = logit[t].rearrange("p (h s) -> p h s", h=A_HEADS)
                dve.wait_ge(expo_ready, t + 1)
                dve.tensor_reduce(row_sum, lg, AX.X, ALU.add)
                dve.drain()
                dve.reciprocal(row_inv, row_sum)
                dve.drain()
                dve.tensor_tensor(lg, lg, row_inv.unsqueeze(2).broadcast_to([P, A_HEADS, s]), ALU.mult).then_inc(prob_ready, 1)
                dve.drain()

            def add_projected(t, c):
                dve.wait_ge(wo_ps, 4 * t + c + 1)
                xs = x_tok[:, t, c * WCOLS:(c + 1) * WCOLS]
                dve.tensor_tensor(xs, xs, wo_at[t][c], ALU.add)
                if c == 3:
                    dve.drain().then_inc(x_ready, 1)

            index_scores(0)
            take_top(0)
            index_scores(1)
            rotary(0, 0)
            take_top(1)
            rotary(0, 1)
            logits(0)
            probs(0)
            swish_of_retention(0)
            decay_scores(0)
            group_norm(0)
            gate_retained(0)
            add_projected(0, 0)
            add_projected(0, 1)
            logits(1)
            for c in range(2, 4):
                add_projected(0, c)

            def heads(p, i, pair=(0, 1)):
                t = p % 2
                both = [(b, j) for b in pair for j in range(2)]
                side = {(b, j): ps_s[:, b, j * P:(j + 1) * P] for b, j in both}
                flat = {b: cand[:, b, :, :].rearrange("p a b -> p (a b)") for b in pair}
                for b in pair:
                    dve.wait_ge(s_ps, i * 2 + (p * P_HEADS + b + 1))
                    dve.sem_inc(topk_on, 1)
                    for j in range(2):
                        dve.max(top_v[:, b, j, 0:8], side[b, j])
                dve.drain()
                for b, j in both:
                    dve.max_index(top_i[:, b, j, 0:8], top_v[:, b, j, 0:8], side[b, j])
                    last = dve.match_replace(rest[:, b, j, :], top_v[:, b, j, 0:8], side[b, j], LOWEST)
                    if j:
                        last.then_inc(s_read, 1)
                dve.drain()
                for b, j in both:
                    dve.max(top_v[:, b, j, 8:16], rest[:, b, j, :])
                dve.drain()
                for b in pair:
                    dve.tensor_tensor(cand[:, b, :, :], top_v[:, b, 0, :].unsqueeze(2).broadcast_to([P, P_TOP, P_TOP]),
                                      top_v[:, b, 1, :].unsqueeze(1).broadcast_to([P, P_TOP, P_TOP]), ALU.add)
                for b, j in both:
                    dve.max_index(top_i[:, b, j, 8:16], top_v[:, b, j, 8:16], rest[:, b, j, :])
                dve.drain()
                for b in pair:
                    dve.max(best_v[:, b, 0:8], flat[b])
                dve.drain()
                for b in pair:
                    dve.max_index(best_i[:, b, 0:8], best_v[:, b, 0:8], flat[b])
                dve.drain()
                for b in pair:
                    dve.match_replace(flat[b], best_v[:, b, 0:8], flat[b], LOWEST)
                dve.drain()
                for b in pair:
                    dve.max(best_v[:, b, 8:16], flat[b])
                dve.drain()
                for b in pair:
                    dve.tensor_scalar(lead[:, b, :], best_v[:, b, :], best_v[:, b, 0:1], None, ALU.subtract).then_inc(lead_ready, 1)
                for b in pair:
                    dve.max_index(best_i[:, b, 8:16], best_v[:, b, 8:16], flat[b])
                dve.drain()
                for b in pair:
                    dve.tensor_scalar(best_ab[:, b, 0, :], best_i[:, b, :], 4, None, ALU.logical_shift_right)
                    dve.tensor_scalar(best_ab[:, b, 1, :], best_i[:, b, :], P_TOP - 1, None, ALU.bitwise_and)
                dve.drain()
                for b in pair:
                    dve.tensor_tensor(onehot[:, b, :, :, :], best_ab[:, b, :, :].unsqueeze(3).broadcast_to([P, 2, P_TOP, P_TOP]),
                                      iota16[:, :].unsqueeze(1).unsqueeze(1).broadcast_to([P, 2, P_TOP, P_TOP]), ALU.is_equal)
                dve.drain()
                for b in pair:
                    dve.tensor_tensor(onehot[:, b, :, :, :], onehot[:, b, :, :, :],
                                      top_i[:, b, :, :].unsqueeze(2).broadcast_to([P, 2, P_TOP, P_TOP]), ALU.mult)
                for b in pair:
                    dve.wait_ge(gate_exp, i * 2 + (p * P_HEADS + b + 1))
                    dve.reciprocal(expo_sum[:, b:b + 1], expo_sum[:, b:b + 1])
                dve.drain()
                for b in pair:
                    dve.tensor_reduce(e12[:, b, :, :], onehot[:, b, :, :, :], AX.X, ALU.add)
                    dve.tensor_scalar(gates[:, t, ds(i * (2 * P_TOP) + b * P_TOP, P_TOP)], expo[:, b, :],
                                      expo_sum[:, b:b + 1], None, ALU.mult)
                dve.drain()
                for b in pair:
                    dve.scalar_tensor_tensor(out=eidx[:, t, ds(i * (2 * P_TOP) + b * P_TOP, P_TOP)], in0=e12[:, b, 0, :],
                                             scalar=float(P), in1=e12[:, b, 1, :], op0=ALU.mult, op1=ALU.add).then_inc(picks_ready, 1)
                dve.drain()

            def expert_round(p, i, between=None):
                t = p % 2
                rounds = PICKS // RING
                xs = x_tok[:, t, 0:HALF]

                def dot(r):
                    dve.wait_ge(gathered[r], i * 16 + 16 * (p * rounds + 1))
                    dve.scalar_tensor_tensor(out=ring[:, r, 0:D], in0=ring[:, r, 0:D], scalar=1.0, in1=h_tok[:, t, :],
                                             op0=ALU.mult, op1=ALU.mult, accum_out=hb[:, r:r + 1]).then_inc(dots_ready, 1)

                def add_v(r):
                    n = p * PICKS + r
                    if r % BATCH == 0:
                        dve.wait_ge(act_ready, i * RING + (n + BATCH))
                    dve.wait_ge(v_added, i * RING + (n + RING))
                    dve.scalar_tensor_tensor(out=xs, in0=ring[:, r, D:D + HALF], scalar=act_v[:, r:r + 1], in1=xs,
                                             op0=ALU.mult, op1=ALU.add).then_inc(v_added, 1)

                for r in range(RING + BATCH):
                    if between:
                        between(r)
                    if r < RING:
                        dot(r)
                    if r >= BATCH:
                        add_v(r - BATCH)

            def close_sum(p):
                dve.wait_ge(v_multiplied, RING + (p + 1) * PICKS)
                dve.tensor_copy(x_tok[:, p % 2, HALF:D], acc).then_inc(x_ready, 1)

            def glu_history(t):
                if t:
                    dve.tensor_copy(glu[:, :, 0:HIST], glu[:, :, P:P + HIST])
                    dve.drain()
                else:
                    dve.wait_ge(small_loaded, 32)
                    dve.memset(glu[:, :, 0:HIST], 0.0)

            def conv_pair(t, q):
                tiles = range(2 * q, 2 * q + 2)
                for c in tiles:
                    dve.wait_ge(sig_ready, t * KD + c + 1)
                    dve.scalar_tensor_tensor(out=glu[:, c, HIST:HIST + P], in0=pm[:, (c % 4) * 512:(c % 4) * 512 + P],
                                             scalar=chan_sb[:, CP_BA + c:CP_BA + c + 1], in1=gate_sig[:, c % 4, :],
                                             op0=ALU.add, op1=ALU.mult).then_inc(glu_ready, 1)
                for w in range(TAPS):
                    for c in tiles:
                        src, dst = glu[:, c, w:w + P], y_t[:, c, :]
                        tap = chan_sb[:, CP_DW + c * TAPS + w:CP_DW + c * TAPS + w + 1]
                        if w == 0:
                            dve.wait_ge(glu_ready, 4 + t * KD + c + 1)
                            step = dve.tensor_scalar(dst, src, tap, chan_sb[:, CP_DWB + c:CP_DWB + c + 1], ALU.mult, ALU.add)
                        else:
                            dve.wait_ge(conv_steps, (4 * t + q) * 2 * TAPS + 2 * (w - 1) + c % 2 + 1)
                            step = dve.scalar_tensor_tensor(out=dst, in0=src, scalar=tap, in1=dst, op0=ALU.mult, op1=ALU.add)
                        step.then_inc(conv_steps, 1)

            def conv_centre(t):
                dve.wait_ge(mu_ps, t + 1)
                dve.tensor_tensor(y_t[:, :, :], y_t[:, :, :], pm[:, 0:P].unsqueeze(1).broadcast_to([P, KD, P]),
                                  ALU.subtract).then_inc(yc_ready, 1)

            def conv_norm(t):
                dve.wait_ge(root_ready, t + 1)
                dve.reciprocal(rstd_y[:, :], rstd_y[:, :])
                dve.drain()
                dve.tensor_tensor(y_t[:, :, :], y_t[:, :, :], rstd_y[:, :].unsqueeze(1).broadcast_to([P, KD, P]), ALU.mult)
                dve.drain()
                for c in range(KD):
                    last = dve.tensor_scalar(y_t[:, c, :], y_t[:, c, :], chan_sb[:, CP_G + c:CP_G + c + 1],
                                             chan_sb[:, CP_B + c:CP_B + c + 1], ALU.mult, ALU.add)
                last.then_inc(u_ready, 1)
                dve.wait_ge(zsig_ready, t + 1)
                dve.tensor_tensor(z_t[:, :, :], z_t[:, :, :], y_t[:, :, :], ALU.mult).then_inc(z_ready, 1)

            def conv_out(t):
                g = GAIN_LOADS.index(("bias", t))
                dve.wait_ge(gain_loaded[g % 2], 16 * (g // 2 + 1))
                dve.tensor_tensor(x_tok[:, t, :], x_tok[:, t, :], gain[:, g % 2, :], ALU.add).then_inc(bias_added, 1)
                dve.drain()
                for c in range(4):
                    n = 4 * t + c
                    dve.wait_ge(w2_ps, n + 1)
                    xs = x_tok[:, t, c * WCOLS:(c + 1) * WCOLS]
                    dve.tensor_tensor(xs, xs, pm[:, c * 512:c * 512 + WCOLS], ALU.add)
                dve.drain().then_inc(x_ready, 1)

            dve.wait_ge(const_ready, 2)
            norm(2)
            probs(1)
            rotary(1, 1)
            heads(0, 0, (0,))
            heads(0, 0, (1,))
            rotary(1, 0)
            decay_scores(1)
            group_norm(1)
            swish_of_retention(1)
            gate_retained(1)
            expert_round(0, 0)
            heads(0, 1)
            expert_round(0, 1)
            heads(0, 2)
            for c in range(4):
                add_projected(1, c)
            expert_round(0, 2)
            heads(0, 3)
            norm(3)
            with dve.Fori(0, 4) as i:
                expert_round(0, i + 3)
                heads(1, i)
            expert_round(0, 7)
            close_sum(0)
            for p in (1, 2):
                t = p - 1
                norm(2 * p + 2)
                glu_history(t)
                expert_round(p, 0)
                conv_pair(t, 0)
                expert_round(p, 1, lambda r: conv_pair(t, 1) if r == 8 else None)
                conv_pair(t, 2)
                expert_round(p, 2, lambda r: conv_pair(t, 3) if r == 12 else None)
                conv_centre(t)
                expert_round(p, 3, lambda r: conv_norm(t) if r == 8 else None)
                conv_out(t)
                norm(2 * p + 3)
                with dve.Fori(0, 3) as i:
                    expert_round(p, i + 4)
                    heads(p + 1, i)
                expert_round(p, 7)
                close_sum(p)
                heads(p + 1, 3)
            norm(8)
            with dve.Fori(0, 8) as i:
                expert_round(3, i)
            close_sum(3)
            norm(9)

        @block.tensor
        def _(pe):
            def norm_h_t(e):
                t = NORMS[e][1]
                pe.wait_ge(h_ready, e + 1)
                for k in range(KD):
                    last = pe.transpose(norm_at(e)[:, k * P:(k + 1) * P], h_tok[:, t, k * P:(k + 1) * P], ident[:, :])
                last.then_inc(h_t_ps, 1)

            def product(dst, lhs, rhs):
                for k in range(KD):
                    last = pe.matmul(dst, lhs(k), rhs(k), start=(k == 0), stop=(k == KD - 1))
                return last

            pe.sem_inc(v_multiplied, RING)
            pe.wait_ge(const_ready, 2)
            norm_h_t(0)
            norm_h_t(1)
            pe.wait_ge(h_t_ready, 2)

            def project(kind, t, before_last=None):
                n = job_of(kind, t)
                part = PROJ[n][2]
                pe.wait_ge(w_in_loaded[part], 16)
                if n >= 4:
                    pe.wait_ge(proj_read[n % 4], n // 4)
                ps, w, h = pm[:, (n % 4) * 512:(n % 4) * 512 + 512], w_part[part], h_in[t]
                if kind == "ckv":
                    product(ps[:, 0:LATENT], lambda k: h[:, k, :], lambda k: w[:, k, 0:LATENT])
                    c0 = C_WI - C_CKV
                    last = product(ps[:, LATENT:LATENT + I_HEADS], lambda k: h[:, k, :], lambda k: w[:, k, c0:c0 + I_HEADS])
                elif kind == "qi":
                    c0 = C_QI - C_CKV
                    for i in range(2):
                        last = product(ps[:, i * P:(i + 1) * P], lambda k: w[:, k, c0 + i * P:c0 + (i + 1) * P], lambda k: h[:, k, :])
                elif kind == "ki":
                    pe.wait_ge(ki_copied, 1)
                    last = product(ps[:, 0:P], lambda k: ki_w[:, k, :], lambda k: h[:, k, :])
                elif kind == "qa":
                    for i in range(4):
                        last = product(ps[:, i * P:(i + 1) * P], lambda k: w[:, k, i * P:(i + 1) * P], lambda k: h[:, k, :])
                elif kind in ("rq", "rk"):
                    for i in range(2):
                        for a in range(2):
                            c0 = i * 2 * R_D + a
                            if before_last and i and a:
                                before_last()
                            last = product(ps[:, (2 * i + a) * P:(2 * i + a + 1) * P], lambda k: w[:, k, c0:c0 + 2 * R_D - 1:2],
                                           lambda k: h[:, k, :])
                else:
                    last = product(ps[:, :], lambda k: h[:, k, :], lambda k: w[:, k, :])
                last.then_inc(proj_ps, 1)

            def transpose_latents():
                n = job_of("c_t", 0)
                pe.wait_ge(proj_read[n % 4], n // 4)
                pe.wait_ge(c_ready, TILES)
                for t in range(TILES):
                    last = pe.transpose(pm[:, (n % 4) * 512 + t * P:(n % 4) * 512 + (t + 1) * P], c_tok[:, t, :], ident[:, :])
                last.then_inc(proj_ps, 1)

            def index_products(t):
                s = P * (t + 1)
                pe.wait_ge(proj_read[job_of("qi", t) % 4], job_of("qi", t) // 4 + 1)
                pe.wait_ge(proj_read[job_of("ki", t) % 4], job_of("ki", t) // 4 + 1)
                if t:
                    pe.wait_ge(rel_ready, t)
                for h in range(I_HEADS):
                    rows = slice((h % 4) * I_DIM, (h % 4 + 1) * I_DIM)
                    c0 = (h // 4) * s
                    last = pe.matmul(side[:, h % 4, c0:c0 + s], qi_t[rows, h // 4, t * P:(t + 1) * P], ki_t[rows, 0:s], start=True, stop=True)
                last.then_inc(idx_ps, 1)

            def retention_scores(t):
                pe.wait_ge(rot_ready, 2 * (t + 1))
                for b in range(2):
                    for h in (b, b + 2):
                        rows = slice(b * 64, b * 64 + 64)
                        for n, s in enumerate((t, 0)[:t + 1]):
                            c0 = (h // 2) * P * (t + 1) + n * P
                            for a in range(2):
                                last = pe.matmul(retention_ps[t][:, b, c0:c0 + P],
                                                 rqk[rows, 1, h // 2, a, s * P:(s + 1) * P], rqk[rows, 0, h // 2, a, t * P:(t + 1) * P],
                                                 start=(a == 0), stop=(a == 1))
                last.then_inc(ret_s_ps, 1)

            def retain(t):
                pe.wait_ge(ret_s_ready, t + 1)
                n = job_of("rv", t)
                pe.wait_ge(proj_read[n % 4], n // 4 + 1)
                for h in range(R_HEADS):
                    dst = retained_ps[t][:, h * R_D:(h + 1) * R_D]
                    v = slice(h * R_D, (h + 1) * R_D)
                    last = pe.matmul(dst, s_t[t][:, head_slot(h), 0:P], rv[:, t, v], start=True, stop=(t == 0))
                    if t:
                        last = pe.matmul(dst, s_t[t][:, head_slot(h), P:2 * P], rv[:, 0, v], start=False, stop=True)
                last.then_inc(ret_ps, 1)

            def transpose_retained(t):
                pe.wait_ge(b_ready, t + 1)
                for h in range(R_HEADS):
                    last = pe.transpose(b_t_at[t][:, h * P:(h + 1) * P], b_tok[t][:, h * R_D:(h + 1) * R_D], ident[:, :])
                last.then_inc(b_t_ps, 1)

            def absorb(t):
                pe.wait_ge(uk_loaded, 48)
                if t:
                    for b in (2, 3):
                        pe.wait_ge(proj_read[b], 3)
                else:
                    pe.wait_ge(rel_ready, 2)
                n = job_of("qa", t)
                pe.wait_ge(proj_read[n % 4], n // 4 + 1)
                for h in range(A_HEADS):
                    rows = slice((h % 2) * A_DIM, (h % 2 + 1) * A_DIM)
                    last = pe.matmul(absorbed_ps[t][:, h % 2, (h // 2) * P:(h // 2 + 1) * P], ukt_sb[rows, h // 2, :],
                                     qa_t[rows, h // 2, t * P:(t + 1) * P], start=True, stop=True)
                last.then_inc(ql_ps, 1)

            def logit_products(t):
                s = P * (t + 1)
                n = job_of("c_t", 0)
                pe.wait_ge(proj_read[n % 4], n // 4 + 1)
                pe.wait_ge(ql_ready, t + 1)
                if t:
                    for n in (job_of("qa", 1), job_of("rk", 0)):
                        pe.wait_ge(proj_read[n % 4], n // 4 + 1)
                for h in range(A_HEADS):
                    q0 = (h % 2) * 4 * P + (h // 2) * P
                    last = pe.matmul(logits_at[t][:, h * s:(h + 1) * s], ql_t[t][:, q0:q0 + P], c_t[:, 0:s], start=True, stop=True)
                last.then_inc(logit_ps, 1)

            def transpose_probs(t):
                s = P * (t + 1)
                pe.wait_ge(prob_ready, t + 1)
                if t:
                    pe.wait_ge(rot_ready, 3)
                for k in range(t + 1):
                    for h in range(A_HEADS):
                        c0 = (k * A_HEADS + h) * P
                        last = pe.transpose(p_t_at[t][:, c0:c0 + P], logit[t][:, h * s + k * P:h * s + (k + 1) * P], ident[:, :])
                last.then_inc(p_t_ps, 1)

            def latent_sums(t):
                pe.wait_ge(p_t_ready, t + 1)
                for half in range(2):
                    for k in range(t + 1):
                        last = pe.matmul(o_at[t][:, half * 512:(half + 1) * 512], c_tok[:, k, :], p_t[t][:, k, half * 512:(half + 1) * 512],
                                         start=(k == 0), stop=(k == t))
                last.then_inc(o_ps, 1)

            def attended_values(t):
                pe.wait_ge(o_ready, t + 1)
                for h in range(A_HEADS):
                    last = pe.matmul(a_at[t][(h % 2) * A_DIM:(h % 2 + 1) * A_DIM, (h // 2) * P:(h // 2 + 1) * P],
                                     uvw_sb[:, h * A_DIM:(h + 1) * A_DIM], o_t[t][:, h * P:(h + 1) * P], start=True, stop=True)
                last.then_inc(a_ps, 1)

            def chunk(n):
                pe.wait_ge(w_loaded[n % WBUF], 16 * (n // WBUF + 1))
                return wbuf[:, n % WBUF, :, :]

            def output_product(t, c):
                pe.wait_ge(a_ready, t + 1)
                pe.wait_ge(b_t_ready, t + 1)
                w = chunk(W_O[t] + c + (t and c // 2 * 2))
                product(wo_at[t][c], lambda k: mix_t[t][:, k, :], lambda k: w[:, k, :]).then_inc(wo_ps, 1)

            for kind, t in (("ckv", 0), ("ckv", 1), ("qi", 0), ("ki", 0), ("qi", 1), ("ki", 1)):
                project(kind, t)
            index_products(0)
            project("qa", 0)
            transpose_latents()
            index_products(1)
            project("rq", 0)
            absorb(0)
            project("rk", 0)
            logit_products(0)
            project("rv", 0)
            project("rg", 0)
            transpose_probs(0)
            retention_scores(0)
            pe.wait_ge(ret_s_ready, 1)
            latent_sums(0)
            retain(0)
            project("qa", 1)
            attended_values(0)
            transpose_retained(0)
            absorb(1)
            output_product(0, 0)
            output_product(0, 1)
            logit_products(1)
            for c in range(2, 4):
                output_product(0, c)
            pe.wait_ge(logit_ready, 2)
            project("rk", 1, lambda: norm_h_t(2))

            def await_h_t(e):
                pe.wait_ge(h_t_ready, e + 1)

            def heads_start(p):
                await_h_t((2, 3, 5, 7)[p])
                if p == 0:
                    pe.wait_ge(small_loaded, 32)

            def queries(p, i, b):
                n, u = W_PHASE[p] + b, p * P_HEADS + b
                if p == 0:
                    n += 2 * max(i - 1, 0)
                pe.wait_ge(w_loaded[b], i * 16 + 16 * (n // 2 + 1))
                pe.wait_ge(s_read, i * 2 + (u + 1))
                for j in range(2):
                    last = product(ps_q[:, b, j * P:(j + 1) * P], lambda k: wbuf[:, b, k, j * P:(j + 1) * P], lambda k: h_t[:, k, :])
                last.then_inc(q_ps, 1)

            def scores(p, i, b):
                u = p * P_HEADS + b
                pe.wait_ge(q_t_ready, i * 2 + (u + 1))
                for j in range(2):
                    last = pe.matmul(ps_s[:, b, j * P:(j + 1) * P], q_t[:, b, j * P:(j + 1) * P], keys_sb[:, p // 2, j, :], start=True, stop=True)
                last.then_inc(s_ps, 1)

            def heads_in_steps(p, i, n):
                if n < 2:
                    queries(p, i, n)
                else:
                    scores(p, i, n - 2)

            def open_sum(p):
                if p:
                    pe.wait_ge(x_ready, (0, 3, 5, 7)[p])
                pe.matmul(acc, ident[:, :], x_tok[:, p % 2, HALF:D], start=True, stop=False)

            def expert_round(p, i, between=None, last=False):
                for r in range(RING):
                    n = p * PICKS + r
                    pe.wait_ge(diag_ready, i * RING + (n + 1))
                    pe.matmul(acc, diag[:, r % (2 * BATCH), :], ring[:, r, D + HALF:2 * D],
                              start=False, stop=(last and r == RING - 1)) \
                        .then_inc(v_multiplied, 1)
                    if between and (r + 1) % BATCH == 0:
                        between(r // BATCH)

            def conv_in(t, c):
                w = chunk(W_CONV[t] + c)
                pe.wait_ge(glu_ready, t * KD + c + 1)
                for j in range(2):
                    last = product(pm[:, (c % 4) * 512 + j * P:(c % 4) * 512 + (j + 1) * P],
                                   lambda k: w[:, k, j * P:(j + 1) * P], lambda k: h_t[:, k, :])
                last.then_inc(pw_ps, 1)

            def conv_mean(t):
                pe.wait_ge(conv_steps, (t + 1) * KD * TAPS)
                product(pm[:, 0:P], lambda k: mean_w[:, :], lambda k: y_t[:, k, :]).then_inc(mu_ps, 1)

            def conv_variance(t):
                pe.wait_ge(ysq_ready, t + 1)
                product(pm[:, P:2 * P], lambda k: mean_w[:, :], lambda k: z_t[:, k, :]).then_inc(var_ps, 1)

            def conv_out(t, c):
                pe.wait_ge(z_ready, t + 1)
                w = chunk(W_CONV[t] + KD + c)
                dst = pm[:, c * 512:c * 512 + WCOLS]
                product(dst, lambda k: z_t[:, k, :], lambda k: w[:, k, :]).then_inc(w2_ps, 1)

            def conv_beside(t, i, b):
                if (i, b) in CONV_INS:
                    conv_in(t, CONV_INS.index((i, b)))
                elif (i, b) == (2, 2):
                    conv_mean(t)
                elif i == 3 and b:
                    for c in ((0,), (1, 2), (3,))[b - 1]:
                        conv_out(t, c)

            heads_start(0)
            queries(0, 0, 0)
            scores(0, 0, 0)
            transpose_probs(1)
            latent_sums(1)
            queries(0, 0, 1)
            attended_values(1)
            scores(0, 0, 1)
            pe.wait_ge(a_ready, 2)
            project("rq", 1)
            project("rv", 1)
            retention_scores(1)
            retain(1)
            project("rg", 1)
            transpose_retained(1)
            open_sum(0)

            def heads_and_output(i, b):
                heads_in_steps(0, i + 1, b)
                if b >= 2:
                    output_product(1, 2 * i + b - 2)

            for i in range(2):
                expert_round(0, i, lambda b: heads_and_output(i, b))
            expert_round(0, 2, lambda b: heads_in_steps(0, 3, b))
            norm_h_t(3)
            heads_start(1)
            with pe.Fori(0, 4) as i:
                expert_round(0, i + 3, lambda b: heads_in_steps(1, i, b))
            expert_round(0, 7, last=True)
            for p in (1, 2):
                t = p - 1
                open_sum(p)
                norm_h_t(2 * p + 2)
                await_h_t(2 * p + 2)
                for i in range(4):
                    expert_round(p, i, lambda b: conv_beside(t, i, b))
                    if i == 2:
                        conv_variance(t)
                norm_h_t(2 * p + 3)
                heads_start(p + 1)
                with pe.Fori(0, 3) as i:
                    expert_round(p, i + 4, lambda b: heads_in_steps(p + 1, i, b))
                expert_round(p, 7, lambda b: heads_in_steps(p + 1, 3, b), last=True)
            open_sum(3)
            with pe.Fori(0, 7) as i:
                expert_round(3, i)
            expert_round(3, 7, last=True)


def rotary_table():
    freq = (1.0 / (np.float32(10000.0) ** np.linspace(0.0, 1.0, R_D // 2, dtype=np.float32))).astype(np.float32)
    ang = (np.tile(freq, 2)[:, None] * np.arange(SEQ, dtype=np.float32)[None, :]).astype(np.float32)
    return np.stack([np.cos(ang), np.sin(ang)], axis=1).astype(np.float32)


def decay_table():
    log_g = np.log1p(-np.exp2(-5.0 - np.arange(R_HEADS)))
    diff = np.arange(P)[None, :] - np.arange(P)[:, None]
    near = np.where(diff[:, None, :] >= 0, np.exp(np.maximum(diff, 0)[:, None, :] * log_g[None, :, None]), 0.0)
    far = np.exp((diff + P)[:, None, :] * log_g[None, :, None])
    return (np.concatenate([near, far], axis=2)[:, [0, 2, 1, 3]] * R_D ** -0.5).astype(np.float32)


def kernel(**inputs):
    import concourse.bacc as bacc
    from concourse.bass_utils import run_bass_kernel_spmd

    a = {k: np.asarray(v) for k, v in inputs.items()}

    def channels(v):
        return v.reshape(-1, P).T

    taps = a["conv_dw"][0].T.reshape(KD, P, TAPS).transpose(1, 0, 2).reshape(P, KD * TAPS)
    arrays = {
        "x": a["x"][0],
        "gains": np.concatenate([a["mix_norm_e"], a["ffn_norm"][0:1], a["mix_norm_o"], a["ffn_norm"][1:2], a["final_norm"][None]]),
        "w_in": a["w_in"][0],
        "kv_norm": a["kv_norm"],
        "uk_t": a["w_uk"][0].transpose(0, 2, 1).reshape(4, P, LATENT).transpose(1, 0, 2),
        "uv_w": a["w_uv"][0].transpose(1, 0, 2).reshape(LATENT, A_HEADS * A_DIM),
        "w_o": a["w_o"][0],
        "rot": rotary_table(),
        "decay": decay_table(),
        "w1": a["conv_w1"][0].reshape(D, 2, KD, P).transpose(0, 2, 1, 3).reshape(D, 2 * D),
        "chan": np.concatenate([taps, channels(a["conv_b1"][0]), channels(a["conv_dw_b"][0]),
                                channels(a["conv_ln_g"][0]), channels(a["conv_ln_b"][0])], axis=1),
        "w2": a["conv_w2"][0],
        "b2": a["conv_b2"],
        "wq": a["peer_wq"],
        "keys_t": a["peer_keys"].transpose(3, 0, 1, 2),
        "experts0": np.concatenate([a["peer_u"][0], a["peer_v"][0]], axis=1),
        "experts1": np.concatenate([a["peer_u"][1], a["peer_v"][1]], axis=1),
    }
    arrays = {f"{n}_dram": np.ascontiguousarray(v) for n, v in arrays.items()}
    nc = bacc.Bacc("TRN2", target_bir_lowering=False, num_devices=1)
    args = [nc.dram_tensor(n, v.shape, mybir.dt.from_np(v.dtype), kind="ExternalInput").ap() for n, v in arrays.items()]
    out = nc.dram_tensor("out_dram", (SEQ, D), mybir.dt.float32, kind="ExternalOutput").ap()
    hybrid_decoder_trunk_kernel(nc, *args, out)
    r = run_bass_kernel_spmd(nc, [arrays], core_ids=[0])
    return r.results[0]["out_dram"].reshape(1, SEQ, D)
```
